# Optimizing a Trainium2 kernel written in Bass

```python
import math
import jax, jax.numpy as jnp
from jax import lax
import numpy as np

D_MODEL = 1024
BATCH = 1
SEQ = 512
DEPTH = 1

N_HEADS_A = D_MODEL // 128
HEAD_DIM_A = 64
A_QK_WIDTH = N_HEADS_A * 2 * HEAD_DIM_A
A_V_WIDTH = N_HEADS_A * 2 * HEAD_DIM_A
N_HEADS_B = D_MODEL // 128
DK_B = 128
DV_B = 128
B_QK_WIDTH = N_HEADS_B * DK_B
B_V_WIDTH = N_HEADS_B * DV_B
CONV_B = 4
CHUNK_B = 64
N_BRANCH = 2
D_FF = ((8 * D_MODEL // 3 + 127) // 128) * 128
CONV_FF = 3
D_PLE = 256
N_BUCKETS = 32
MAX_DISTANCE = 128
Q_BLOCK = 128
EPS = 1e-6
NEG_INF = -1e30

SPLITS = (A_QK_WIDTH, A_QK_WIDTH, A_V_WIDTH, B_QK_WIDTH, B_QK_WIDTH, B_V_WIDTH, B_V_WIDTH, N_HEADS_B, N_HEADS_B, N_BRANCH * D_MODEL)
D_IN = sum(SPLITS)

kernel_name = "hybrid_diffattn_gdn_convffn_block"

def rmsnorm(x, g):
    xf = x.astype(jnp.float32)
    y = xf * lax.rsqrt(jnp.mean(xf * xf, axis=-1, keepdims=True) + EPS)
    return (y * g.astype(jnp.float32)).astype(x.dtype)

def l2norm(x):
    xf = x.astype(jnp.float32)
    return xf * lax.rsqrt(jnp.sum(xf * xf, axis=-1, keepdims=True) + EPS)

def causal_dwconv(x, w):
    K = w.shape[0]
    S = x.shape[1]
    xp = jnp.pad(x, ((0, 0), (K - 1, 0), (0, 0)))
    y = xp[:, 0:S] * w[0]
    for j in range(1, K):
        y = y + xp[:, j:j + S] * w[j]
    return y

def rel_bucket(rel):
    n = jnp.maximum(rel, 0)
    max_exact = N_BUCKETS // 2
    nf = jnp.maximum(n, 1).astype(jnp.float32)
    large = max_exact + (jnp.log(nf / max_exact) / math.log(MAX_DISTANCE / max_exact) * (N_BUCKETS - max_exact)).astype(jnp.int32)
    large = jnp.minimum(large, N_BUCKETS - 1)
    return jnp.where(n < max_exact, n, large)

def diff_attention(q, k, v, lam, bias_table):
    B, S, H, _, d = q.shape
    nb = S // Q_BLOCK
    qb = q.reshape(B, nb, Q_BLOCK, H, 2, d).transpose(1, 0, 2, 3, 4, 5)
    k_pos = jnp.arange(S)

    def block(args):
        idx, q_blk = args
        q_pos = idx * Q_BLOCK + jnp.arange(Q_BLOCK)
        rel = q_pos[:, None] - k_pos[None, :]
        bias = bias_table[rel_bucket(rel)].astype(jnp.float32).transpose(2, 0, 1)
        logits = jnp.einsum('bqhjd,bkhjd->bhjqk', q_blk, k, preferred_element_type=jnp.float32)
        logits = logits + bias[None, :, None]
        logits = jnp.where((rel >= 0)[None, None, None], logits, NEG_INF)
        probs = jax.nn.softmax(logits, axis=-1)
        w = probs[:, :, 0] - lam * probs[:, :, 1]
        return jnp.einsum('bhqk,bkhe->bqhe', w.astype(v.dtype), v)

    out = lax.map(block, (jnp.arange(nb), qb))
    return out.transpose(1, 0, 2, 3, 4).reshape(B, S, H, 2 * d)

def gated_delta_rule(q, k, v, g, beta):
    B, S, H, dk = q.shape
    dv = v.shape[-1]
    C = CHUNK_B
    N = S // C

    def to_chunks(t):
        return t.reshape(B, N, C, H, t.shape[-1]).transpose(1, 0, 3, 2, 4)

    q, k, v = to_chunks(q), to_chunks(k), to_chunks(v)
    g = jnp.cumsum(g.reshape(B, N, C, H).transpose(1, 0, 3, 2), axis=-1)
    beta = beta.reshape(B, N, C, H).transpose(1, 0, 3, 2)
    tril = jnp.tril(jnp.ones((C, C), dtype=bool))
    strict = jnp.tril(jnp.ones((C, C), dtype=bool), -1)
    decay = jnp.exp(jnp.where(tril, g[..., :, None] - g[..., None, :], -jnp.inf))
    k_beta = k * beta[..., None]
    v_beta = v * beta[..., None]
    kkT = jnp.einsum('nbhid,nbhjd->nbhij', k_beta, k)
    A = jnp.eye(C, dtype=jnp.float32) + jnp.where(strict, kkT * decay, 0.0)
    rhs = jnp.concatenate([v_beta, k_beta * jnp.exp(g)[..., None]], axis=-1)
    sol = lax.linalg.triangular_solve(A, rhs, left_side=True, lower=True, unit_diagonal=True)
    u = sol[..., :dv]
    w = sol[..., dv:]
    attn_intra = jnp.where(tril, jnp.einsum('nbhid,nbhjd->nbhij', q, k) * decay, 0.0)

    def step(state, inp):
        q_c, k_c, u_c, w_c, g_c, a_c = inp
        v_new = u_c - w_c @ state
        o = (q_c * jnp.exp(g_c)[..., None]) @ state + a_c @ v_new
        g_last = g_c[..., -1]
        k_dec = k_c * jnp.exp(g_last[..., None] - g_c)[..., None]
        state = state * jnp.exp(g_last)[..., None, None] + jnp.swapaxes(k_dec, -1, -2) @ v_new
        return state, o

    s0 = jnp.zeros((B, H, dk, dv), dtype=jnp.float32)
    _, o = lax.scan(step, s0, (q, k, u, w, g, attn_intra))
    return o.transpose(1, 0, 3, 2, 4).reshape(B, S, H, dv)

def setup_inputs(seed: int = 0) -> dict:
    key = jax.random.key(seed)
    ks = jax.random.split(key, 26)
    f32 = jnp.float32
    nrm = lambda k, shape, s: jax.random.normal(k, shape, f32) * s
    gain = lambda k, shape: 1.0 + 0.02 * jax.random.normal(k, shape, f32)
    dt = jnp.exp(jax.random.uniform(ks[10], (DEPTH, N_HEADS_B), f32, math.log(1e-3), math.log(1e-1)))
    return {
        "x": nrm(ks[0], (BATCH, SEQ, D_MODEL), 1.0),
        "p": nrm(ks[1], (DEPTH, BATCH, SEQ, D_PLE), 1.0),
        "w_in": nrm(ks[2], (DEPTH, D_MODEL, D_IN), D_MODEL ** -0.5),
        "attn_norm": gain(ks[3], (DEPTH, D_MODEL)),
        "qnorm_a": gain(ks[4], (DEPTH, HEAD_DIM_A)),
        "knorm_a": gain(ks[5], (DEPTH, HEAD_DIM_A)),
        "lam_a": nrm(ks[6], (DEPTH, 4, HEAD_DIM_A), 0.1),
        "subln_a": gain(ks[7], (DEPTH, 2 * HEAD_DIM_A)),
        "rel_bias": nrm(ks[8], (N_BUCKETS, N_HEADS_A), 0.3),
        "conv_b": nrm(ks[9], (DEPTH, CONV_B, 2 * B_QK_WIDTH + B_V_WIDTH), CONV_B ** -0.5),
        "a_log_b": jnp.log(jax.random.uniform(ks[11], (DEPTH, N_HEADS_B), f32, 1.0, 16.0)),
        "dt_bias_b": dt + jnp.log(-jnp.expm1(-dt)),
        "onorm_b": gain(ks[12], (DEPTH, DV_B)),
        "w_br_a": nrm(ks[13], (DEPTH, A_V_WIDTH, D_MODEL), A_V_WIDTH ** -0.5),
        "w_br_b": nrm(ks[14], (DEPTH, B_V_WIDTH, D_MODEL), B_V_WIDTH ** -0.5),
        "w_out": nrm(ks[15], (DEPTH, D_MODEL, D_MODEL), D_MODEL ** -0.5),
        "ffn_norm": gain(ks[16], (DEPTH, D_MODEL)),
        "w_up": nrm(ks[17], (DEPTH, D_MODEL, 2 * D_FF), D_MODEL ** -0.5),
        "conv_ff": nrm(ks[18], (DEPTH, CONV_FF, 2 * D_FF), CONV_FF ** -0.5),
        "conv_ff_bias": nrm(ks[19], (DEPTH, 2 * D_FF), 0.01),
        "w_down": nrm(ks[20], (DEPTH, D_FF, D_MODEL), D_FF ** -0.5),
        "ple_norm": gain(ks[21], (DEPTH, D_MODEL)),
        "w_ple_gate": nrm(ks[22], (DEPTH, D_MODEL, D_MODEL), D_MODEL ** -0.5),
        "w_ple_proj": nrm(ks[23], (DEPTH, D_PLE, D_MODEL), D_PLE ** -0.5),
    }

def reference(x, p, w_in, attn_norm, qnorm_a, knorm_a, lam_a, subln_a, rel_bias, conv_b, a_log_b, dt_bias_b, onorm_b, w_br_a, w_br_b, w_out, ffn_norm, w_up, conv_ff, conv_ff_bias, w_down, ple_norm, w_ple_gate, w_ple_proj):
    Bsz, S, _ = x.shape
    cuts = np.cumsum(SPLITS)[:-1].tolist()
    for i in range(DEPTH):
        lam_init = 0.8 - 0.6 * math.exp(-0.3 * i)
        h = rmsnorm(x, attn_norm[i])
        proj = h @ w_in[i]
        qa, ka, va, qb, kb, vb, zb, bb, ab, gl = jnp.split(proj, cuts, axis=-1)

        qa = rmsnorm(qa.reshape(Bsz, S, N_HEADS_A, 2, HEAD_DIM_A), qnorm_a[i]) * (HEAD_DIM_A ** -0.5)
        ka = rmsnorm(ka.reshape(Bsz, S, N_HEADS_A, 2, HEAD_DIM_A), knorm_a[i])
        lq = lam_a[i].astype(jnp.float32)
        lam = jnp.exp(jnp.sum(lq[0] * lq[1])) - jnp.exp(jnp.sum(lq[2] * lq[3])) + lam_init
        oa = diff_attention(qa, ka, va.reshape(Bsz, S, N_HEADS_A, 2 * HEAD_DIM_A), lam, rel_bias)
        oa = (rmsnorm(oa, subln_a[i]) * (1.0 - lam_init)).reshape(Bsz, S, A_V_WIDTH)

        qkv = jax.nn.silu(causal_dwconv(jnp.concatenate([qb, kb, vb], axis=-1), conv_b[i]))
        qb, kb, vb = jnp.split(qkv, [B_QK_WIDTH, 2 * B_QK_WIDTH], axis=-1)
        qb = l2norm(qb.reshape(Bsz, S, N_HEADS_B, DK_B)) * (DK_B ** -0.5)
        kb = l2norm(kb.reshape(Bsz, S, N_HEADS_B, DK_B))
        vb = vb.reshape(Bsz, S, N_HEADS_B, DV_B).astype(jnp.float32)
        beta = jax.nn.sigmoid(bb.astype(jnp.float32))
        g = -jnp.exp(a_log_b[i].astype(jnp.float32)) * jax.nn.softplus(ab.astype(jnp.float32) + dt_bias_b[i].astype(jnp.float32))
        ob = gated_delta_rule(qb, kb, vb, g, beta).astype(x.dtype)
        ob = (rmsnorm(ob, onorm_b[i]) * jax.nn.silu(zb.reshape(Bsz, S, N_HEADS_B, DV_B))).reshape(Bsz, S, B_V_WIDTH)

        gates = jax.nn.sigmoid(gl.reshape(Bsz, S, N_BRANCH, D_MODEL))
        mixed = gates[:, :, 0] * (oa @ w_br_a[i]) + gates[:, :, 1] * (ob @ w_br_b[i])
        x = x + mixed @ w_out[i]

        h = rmsnorm(x, ffn_norm[i])
        u = causal_dwconv(h @ w_up[i], conv_ff[i]) + conv_ff_bias[i]
        ug, uv = jnp.split(u, 2, axis=-1)
        x = x + (jax.nn.silu(ug) * uv) @ w_down[i]

        h = rmsnorm(x, ple_norm[i])
        x = x + jax.nn.sigmoid(h @ w_ple_gate[i]) * (p[i] @ w_ple_proj[i])
    return x


_drawn_inputs = setup_inputs


def setup_inputs(seed=0):
    import zlib

    import numpy as np

    out = dict(_drawn_inputs(seed))
    spreads = {}
    factors = {'attn_norm': 3.555,
     'qnorm_a': 7.974,
     'knorm_a': 6.906,
     'subln_a': 52.531,
     'onorm_b': 42.52,
     'ffn_norm': 12.279,
     'conv_ff_bias': 24.311,
     'ple_norm': 200.0,
     'rel_bias': 4.738,
     'p': 8.0,
     'w_ple_gate': 8.0,
     'w_ple_proj': 8.0}
    for name, (base, spread) in spreads.items():
        noise = np.random.default_rng([zlib.crc32(name.encode()), seed]).standard_normal(out[name].shape)
        drawn = base * np.exp(spread * noise) if base else spread * noise
        out[name] = __import__('jax').numpy.asarray(drawn.astype(out[name].dtype))
    for name, factor in factors.items():
        out[name] = (out[name] * factor).astype(out[name].dtype)
    return out
```

```python
import math
from contextlib import ExitStack

import numpy as np

import concourse.bass as bass
from concourse import mybir

F32 = mybir.dt.float32
F32R = mybir.dt.float32r
ALU = mybir.AluOpType
ACT = mybir.ActivationFunctionType
AX_X = mybir.AxisListType.X

P = 128
T = 512
NT = T // P
D = 1024
KD = D // P
H = 8
CH = 64
NC = T // CH
LEVELS = (1, 2, 4, 8, 16, 32)
FF = 2816
KF = FF // P
PLE = 256
KP = PLE // P
EPS = 1e-6
NEG = -1e30
LAM_INIT = 0.8 - 0.6 * math.exp(0.0)
COLS = {"qa": 0, "ka": D, "va": 2 * D, "qb": 3 * D, "kb": 4 * D, "vb": 5 * D, "zb": 6 * D,
        "ba": 7 * D, "g0": 7 * D + 16, "g1": 8 * D + 16}

C_ID, C_FLIP, C_CUM, C_HALF, C_ONES, C_MASK, C_LEVEL, C_HOT = 0, 1, 2, 3, 4, 5, 6, 12
CONST_COLS = C_HOT * P + 384
LINE = 384

PA_ATTN, PA_FFN, PA_PLE, PA_CONV, PA_QN, PA_KN, PA_SUB, PA_ON = 0, 8, 16, 24, 120, 121, 122, 123
PA_TAP = (128, 128 + 44, 256)
PA_FBIAS = 256 + 44


def constants():
    c = np.zeros((P, CONST_COLS), np.float32)
    j, i = np.meshgrid(np.arange(P), np.arange(P), indexing="ij")
    same = (j // CH) == (i // CH)

    def put(n, a):
        c[:, n * P:(n + 1) * P] = a

    put(C_ID, j == i)
    put(C_FLIP, j + i == P - 1)
    put(C_CUM, same & (j <= i))
    put(C_HALF, same)
    put(C_ONES, np.ones((P, P)))
    put(C_MASK, np.where(same & (j <= i), 0.0, NEG))
    for n, m in enumerate(LEVELS):
        put(C_LEVEL + n, (j // (2 * m) == i // (2 * m)) & (j // m % 2 == 0) & (i // m % 2 == 1))
    r = 255 - np.arange(LINE)
    n = np.maximum(r, 0)
    big = 16 + (np.log(np.maximum(n, 1) / 16) / math.log(128 / 16) * 16).astype(np.int64)
    bucket = np.where(n < 16, n, np.minimum(big, 31))
    hot = np.zeros((33, LINE), np.float32)
    hot[np.where(r >= 0, bucket, 32), np.arange(LINE)] = 1.0
    hot[31] -= 1.0
    c[0:33, C_HOT * P:] = hot
    return c


class Chunk:

    def __init__(self, number, slot, arrival, bank, uses):
        self.number = number
        self.slot = slot
        self.arrival = arrival
        self.bank = bank
        self.uses = uses


class Segment:

    def __init__(self, stream, turns, slots, banks):
        self.first, self.turns, self.slots, self.banks = stream.count, turns, slots, banks
        self.slot0, self.bank0 = dict(stream.slot), dict(stream.bank)
        stream.count += turns * len(slots)
        for s in slots:
            stream.slot[s] = stream.slot.get(s, 0) + turns
        for b in banks:
            stream.bank[b] = stream.bank.get(b, 0) + turns

    def at(self, n, turn=0):
        s, b = self.slots[n], self.banks[n]
        return Chunk(turn * len(self.slots) + (self.first + n), s,
                     turn * self.slots.count(s) + (self.slot0.get(s, 0) + self.slots[:n].count(s) + 1),
                     b, turn * self.banks.count(b) + (self.bank0.get(b, 0) + self.banks[:n].count(b)))


class Stream:

    def __init__(self):
        self.count, self.slot, self.bank = 0, {}, {3: 1}
        self.ba = Segment(self, 1, [0], [0])
        self.first = Segment(self, 1, [1, 2, 3], [1, 2, 0])
        self.heads = Segment(self, H - 1, [0, 1, 2, 0, 1, 2, 3], [0, 1, 2, 0, 1, 2, 0])
        self.last = Segment(self, 1, [0, 1, 2, 3], [0, 1, 2, 0])
        four = [0, 1, 2, 3]
        self.mix = Segment(self, KD, four, four)
        self.out = Segment(self, KD // 4, four, four)
        self.up = [None] * 3
        self.down = [None] * 3
        for name, n in FFN_ORDER:
            if name == "up":
                self.up[n] = Segment(self, FFN_PARTS[n] // 2, four, four)
            else:
                self.down[n] = Segment(self, KD // 4, four, four)
        self.ple = Segment(self, KD // 2, four, four)


FFN_PARTS = (8, 8, 6)
FFN_FIRST = (0, 8, 16)
FFN_ORDER = (("up", 0), ("up", 1), ("down", 0), ("up", 2), ("down", 1), ("down", 2))
FFN_HALF = (0, 1, 0)


def build(nc, x, p, w_in, attn_norm, qnorm_a, knorm_a, lam_a, subln_a, rel_bias, conv_b, a_log_b,
          dt_bias_b, onorm_b, w_br_a, w_br_b, w_out, ffn_norm, w_up, conv_ff, conv_ff_bias, w_down,
          ple_norm, w_ple_gate, w_ple_proj, consts, out):
    stream = Stream()
    ctx = ExitStack()
    with ctx:
        def sb(name, shape, dt=F32, stack=ctx):
            return stack.enter_context(nc.sbuf_tensor(name, shape, dt))

        sems = {}

        def sem(name):
            if name not in sems:
                sems[name] = ctx.enter_context(nc.semaphore(name))
            return sems[name]

        raw = [sb(f"w_raw{s}", [P, KD, P]) for s in range(4)]
        whi = [sb(f"w_hi{s}", [P, KD, P], F32R) for s in range(4)]
        wlo = [sb(f"w_lo{s}", [P, KD, P], F32R) for s in range(4)]
        hn_hi = sb("hn_hi", [P, KD, T], F32R)
        hn_lo = sb("hn_lo", [P, KD, T], F32R)
        sq = sb("sq", [P, C_HOT * P])
        pt = sb("pt", [P, 3 * P])
        sm = sb("sm", [P, 64])

        def const(n):
            return sq[:, n * P:(n + 1) * P]

        ident, flip, cum, half, ones, mask = map(const, range(6))

        room = ExitStack()
        mx_hi = sb("mx_hi", [P, KD, T], F32R, room)
        mx_lo = sb("mx_lo", [P, KD, T], F32R, room)
        room.close()
        room = ExitStack()
        u0, u1, s0, tn = (sb(n, [P, T], F32, room) for n in ("u0", "u1", "s0", "tn"))
        p_tok = sb("p_tok", [P, NT, PLE], F32, room)
        p_hi = sb("p_hi", [P, KP, T], F32R, room)
        p_lo = sb("p_lo", [P, KP, T], F32R, room)
        room.close()
        o_a = sb("o_a", [P, H, T])
        o_b = sb("o_b", [P, H, T])
        ws = ExitStack()
        bias = sb("bias", [P, H, 256], F32, ws)
        gates = sb("gates", [P, 12, NT, H], F32, ws)
        qa_raw, ka_raw, va_raw, qa, ka, va = (
            sb(n, [P, T], F32, ws) for n in ("qa_raw", "ka_raw", "va_raw", "qa", "ka", "va"))
        pr = [sb(f"pr{j}", [P, T], F32, ws) for j in range(2)]
        wT = sb("wT", [P, NT, T], F32, ws)
        sqr = [sb(f"sqr{n}", [P, T], F32, ws) for n in range(2)]
        first = ExitStack()
        x_tok = sb("x_tok", [P, NT, D], F32, first)
        prow = sb("prow", [P, 3, P], F32, first)
        hot = sb("hot", [33, LINE], F32, first)
        tab = sb("tab", [33, H], F32, first)
        line = sb("line", [H, LINE], F32, first)
        slope = sb("slope", [P, H, 256], F32, first)
        lamr = sb("lamr", [P, 4, 64], F32, first)
        lamp = sb("lamp", [P, 2, 64], F32, first)
        ba_sb = sb("ba_sb", [16, T], F32, first)
        junk = sb("junk", [P, D], F32, first)
        alog = sb("alog", [P, H], F32, first)
        dtb = sb("dtb", [P, H], F32, first)
        first.close()
        qb, kb, vb, zb = (sb(n, [P, T], F32, ws) for n in ("qb", "kb", "vb", "zb"))
        silu = sb("silu", [P, T], F32, ws)
        sqb = [sb(f"sqb{n}", [P, T], F32, ws) for n in range(2)]
        gcol, bcol = sb("gcol", [P, NT, P], F32, ws), sb("bcol", [P, NT, P], F32, ws)
        qeg, eg, dec, decb, lt, at_ = (
            sb(n, [P, NT, P], F32, ws) for n in ("qeg", "eg", "dec", "decb", "lt", "at_"))
        ct = [sb(f"ct{n}", [P, NT, P], F32, ws) for n in range(2)]
        xi, xt, ui = (sb(n, [P, NT, P], F32, ws) for n in ("xi", "xt", "ui"))
        vbt, kbe, kdec = (sb(n, [P, NT, P], F32, ws) for n in ("vbt", "kbe", "kdec"))
        state, vnew = sb("state", [P, P], F32, ws), sb("vnew", [P, P], F32, ws)
        ast = sb("ast", [P, 16], F32, ws)
        wt_, us = ui, vbt
        ws.close()
        ws = ExitStack()
        oa_hi, oa_lo, ob_hi, ob_lo = (
            sb(n, [P, H, T], F32R, ws) for n in ("oa_hi", "oa_lo", "ob_hi", "ob_lo"))
        x_back = sb("x_back", [P, NT, D], F32, ws)
        sg = [sb(f"sg{n}", [P, T], F32, ws) for n in range(2)]
        ws.close()
        ws = ExitStack()
        x1 = sb("x1", [P, KD, T], F32, ws)
        late = ExitStack()
        fa_hi = sb("fa_hi", [P, 16, T], F32R, late)
        fa_lo = sb("fa_lo", [P, 16, T], F32R, late)
        sqn = sb("sqn", [P, T], F32, late)
        rs = sb("rs", [P, T], F32, late)
        late.close()
        late = ExitStack()
        y_tok = sb("y_tok", [P, NT, D], F32, late)
        yg, yT = sb("yg", [P, T], F32, late), sb("yT", [P, T], F32, late)
        late.close()
        ws.close()

        bank = [ctx.enter_context(nc.psum_tensor(f"bank{b}", [P, T], F32)) for b in range(8)]

        def tiles(b):
            return bank[b][:, :].rearrange("p (t c) -> p t c", c=P)

        dram_line = nc.dram_tensor("bias_line", (H, LINE), F32, kind="Internal").ap()

        w_in0, w_up0, w_down0, gate0, proj0 = w_in[0], w_up[0], w_down[0], w_ple_gate[0], w_ple_proj[0]
        bra0, brb0, wout0 = w_br_a[0], w_br_b[0], w_out[0]
        ss0, rs0, lam_s, nlam, gq8, gsub, alexp = (sm[:, 0:4], sm[:, 4:8], sm[:, 8:10], sm[:, 10:11],
                                                   sm[:, 11:12], sm[:, 12:13], sm[:, 16:24])
        lnx = sm[:, 24:28]
        (G_B, G_A, G_BETA, G_G, G_CUM, G_SUM, G_NEG, G_EXP, G_BEG, G_KD, G_T, G_U) = range(12)

        def gt(n):
            return gates[:, n, :, :]

        def gcols(n, h):
            return gates[:, n, :, bass.ds(h, 1)]

        def dyn(t, i):
            return t[:, bass.ds(i, 1), :].rearrange("p a t -> p (a t)")

        def col(n, i=None):
            return pt[:, n:n + 1] if i is None else pt[:, bass.ds(i + n, 1)]

        arrived = [sem(f"w_arrived{s}") for s in range(4)]
        high_ready, low_ready, product_ready = sem("w_high"), sem("w_low"), sem("product")
        bank_free = [sem(f"bank_read{b}") for b in range(4)]

        block = ctx.enter_context(nc.Block())

        @block.sync
        def _(sp):
            def load(c, w, col0, k=KD, row0=0):
                if not isinstance(c.number, int):
                    split = sp.to_reg(c.number - 2)
                    sp.wait_ge(sem("consts_in"), 16)
                    sp.wait_ge(low_ready, split)
                elif c.number > 2:
                    sp.wait_ge(low_ready, c.number - 2)
                src = w[row0:row0 + k * P, bass.ds(col0, P)].rearrange("(k p) n -> p k n", p=P)
                sp.dma_start(raw[c.slot][:, 0:k, :], src).then_inc(arrived[c.slot], 16)

            for t in range(NT):
                sp.dma_start(x_tok[:, t, :], x[0, t * P:(t + 1) * P, :]).then_inc(sem(f"x_in{t}"), 16)
                if t == 0:
                    sp.dma_start(sq[:, :], consts[:, 0:C_HOT * P]).then_inc(sem("consts_in"), 16)
            rows = [
                (0, PA_ATTN, attn_norm[0].rearrange("(r c) -> r c", c=P)),
                (0, PA_FFN, ffn_norm[0].rearrange("(r c) -> r c", c=P)),
                (0, PA_PLE, ple_norm[0].rearrange("(r c) -> r c", c=P)),
                (0, PA_CONV, conv_b[0].rearrange("j (r c) -> (j r) c", c=P)),
                (0, PA_SUB, subln_a),
                (0, PA_ON, onorm_b),
                (1, 0, conv_ff[0, 0:2].rearrange("j (r c) -> (j r) c", c=P)),
                (2, 0, conv_ff[0, 2:3].rearrange("j (r c) -> (j r) c", c=P)),
                (2, 2 * KF, conv_ff_bias[0].rearrange("(r c) -> r c", c=P)),
            ]
            for plane, row, src in rows:
                sp.dma_start(prow[row:row + src.shape[0], plane, :], src).then_inc(sem("params_in"), 16)
            for half_ in range(2):
                for row, src in ((PA_QN, qnorm_a), (PA_KN, knorm_a)):
                    sp.dma_start(prow[row:row + 1, 0, half_ * 64:half_ * 64 + 64], src).then_inc(sem("params_in"), 16)
            sp.dma_start(hot[:, :], consts[0:33, C_HOT * P:]).then_inc(sem("small_in"), 16)
            sp.dma_start(tab[0:32, :], rel_bias).then_inc(sem("small_in"), 16)
            sp.dma_start(lamr[:, :, :], lam_a[0].partition_broadcast(P)).then_inc(sem("small_in"), 16)
            sp.dma_start(alog[:, :], a_log_b[0].partition_broadcast(P)).then_inc(sem("small_in"), 16)
            sp.dma_start(dtb[:, :], dt_bias_b[0].partition_broadcast(P)).then_inc(sem("small_in"), 16)

            load(stream.ba.at(0), w_in0, COLS["ba"])
            for n, name in enumerate(("qa", "ka", "va")):
                load(stream.first.at(n), w_in0, COLS[name])
            sp.wait_ge(sem("line_ready"), 1)
            sp.dma_start(dram_line, line[:, :]).then_inc(sem("line_out"), 16)
            sp.wait_ge(sem("line_out"), 16)
            skew = bass.AP(tensor=dram_line.tensor, offset=0, ap=[[1, P], [LINE, H], [1, 256]])
            sp.dma_start(slope[:, :, :], skew).then_inc(sem("slope_in"), 16)
            with sp.Fori(0, H - 1) as h:
                for n, name in enumerate(("qb", "kb", "vb", "zb")):
                    load(stream.heads.at(n, h), w_in0, h * P + COLS[name])
                for n, name in enumerate(("qa", "ka", "va")):
                    load(stream.heads.at(4 + n, h), w_in0, h * P + (COLS[name] + P))
            for n, name in enumerate(("qb", "kb", "vb", "zb")):
                load(stream.last.at(n), w_in0, (H - 1) * P + COLS[name])
            with sp.Fori(0, KD) as n:
                load(stream.mix.at(0, n), w_in0, n * P + COLS["g0"])
                load(stream.mix.at(1, n), w_in0, n * P + COLS["g1"])
                load(stream.mix.at(2, n), bra0, n * P)
                load(stream.mix.at(3, n), brb0, n * P)
            sp.wait_ge(sem("ob_done"), H + 1)
            for t in range(NT):
                sp.dma_start(x_back[:, t, :], x[0, t * P:(t + 1) * P, :]).then_inc(sem("x_back_in"), 16)
            with sp.Fori(0, KD // 4) as n:
                for q in range(4):
                    load(stream.out.at(q, n), wout0, n * (4 * P) + q * P)
            for name, part in FFN_ORDER:
                if name == "up":
                    with sp.Fori(0, FFN_PARTS[part] // 2) as n:
                        for q in range(4):
                            first = (FFN_FIRST[part] + q // 2) * P + (q % 2) * FF
                            load(stream.up[part].at(q, n), w_up0, n * (2 * P) + first)
                    if part == 0:
                        sp.wait_ge(product_ready, stream.up[0].first)
                        sp.dma_start(p_tok[:, :, :], p[0, 0].rearrange("(t q) c -> q t c", q=P)).then_inc(sem("p_in"), 16)
                else:
                    with sp.Fori(0, KD // 4) as n:
                        for q in range(4):
                            load(stream.down[part].at(q, n), w_down0, n * (4 * P) + q * P,
                                 FFN_PARTS[part], FFN_FIRST[part] * P)
            with sp.Fori(0, KD // 2) as n:
                for q in range(4):
                    c = stream.ple.at(q, n)
                    if q % 2 == 0:
                        load(c, gate0, n * (2 * P) + (q // 2) * P)
                    else:
                        load(c, proj0, n * (2 * P) + (q // 2) * P, KP)
            for t in range(NT):
                sp.wait_ge(sem("y_ready"), KD)
                sp.dma_start(out[0, t * P:(t + 1) * P, :], y_tok[:, t, :]).then_inc(sem("stored"), 16)
            sp.wait_ge(sem("stored"), 16 * NT)

        @block.gpsimd
        def _(pool):
            def split(c, k=KD):
                loads, products = c.arrival * 16, c.number - 2
                if not isinstance(c.number, int):
                    loads, products = pool.to_reg(loads), pool.to_reg(products)
                pool.wait_ge(sem("consts_in"), 16)
                pool.wait_ge(arrived[c.slot], loads)
                if not isinstance(c.number, int) or c.number > 2:
                    pool.wait_ge(product_ready, products)
                pool.tensor_copy(whi[c.slot][:, 0:k, :], raw[c.slot][:, 0:k, :]).then_inc(high_ready, 1)
                pool.wait_ge(high_ready, c.number + 1)
                pool.tensor_tensor(wlo[c.slot][:, 0:k, :], raw[c.slot][:, 0:k, :],
                                   whi[c.slot][:, 0:k, :].bitcast(F32), ALU.subtract).then_inc(low_ready, 1)

            split(stream.ba.at(0))
            for n in range(3):
                split(stream.first.at(n))
            with pool.Fori(0, H - 1) as h:
                for n in range(7):
                    split(stream.heads.at(n, h))
            for n in range(4):
                split(stream.last.at(n))
            segments = [(stream.mix, [KD] * 4), (stream.out, [KD] * 4)]
            for name, part in FFN_ORDER:
                if name == "up":
                    segments.append((stream.up[part], [KD] * 4))
                else:
                    segments.append((stream.down[part], [FFN_PARTS[part]] * 4))
            segments.append((stream.ple, [KD, KP] * 2))
            for seg, ks in segments:
                with pool.Fori(0, seg.turns) as n:
                    for q in range(4):
                        split(seg.at(q, n), ks[q])

        @block.tensor
        def _(pe):
            for name in ("a_turned", "a_scores",):
                pe.sem_inc(sem(name), 1)
            def gemm(c, x_hi, x_lo, k=KD, x0=0, more=None, signal=True):
                pe.wait_ge(low_ready, c.number + 1)
                if not isinstance(c.uses, int) or c.uses > 0:
                    pe.wait_ge(bank_free[c.bank], c.uses)
                acc = bank[c.bank][:, :]
                for i in range(k):
                    for n, (w, xx) in enumerate(((whi, x_hi), (whi, x_lo), (wlo, x_hi))):
                        last = i == k - 1 and n == 2
                        mm = pe.matmul(acc, w[c.slot][:, i, :], xx[:, x0 + i, :],
                                       start=(i == 0 and n == 0), stop=last)
                    if i < k - 1:
                        yield
                if more is not None:
                    mm = more(acc)
                mm.then_inc(product_ready, 1)
                yield

            def run(*gens):
                for g in gens:
                    for _ in g:
                        pass

            class Fill:

                def __init__(self, *gens):
                    self.gens = list(gens)

                def step(self, n=1):
                    for _ in range(n):
                        while self.gens:
                            try:
                                next(self.gens[0])
                                break
                            except StopIteration:
                                self.gens.pop(0)

                def rest(self):
                    while self.gens:
                        self.step()

            pe.wait_ge(sem("consts_in"), 16)
            pe.wait_ge(sem("params_in"), 16 * 13)
            pe.wait_ge(sem("small_in"), 16 * 5)
            pe.wait_ge(sem("tab_set"), 1)
            pe.transpose(bank[7][:, 0:124], prow[0:124, 0, :], ident[0:124, 0:124])
            pe.transpose(bank[7][:, P:P + 88], prow[0:88, 1, :], ident[0:88, 0:88])
            pe.transpose(bank[7][:, 2 * P:2 * P + 88], prow[0:88, 2, :], ident[0:88, 0:88]).then_inc(sem("params_T"), 1)
            pe.matmul(bank[6][0:H, 0:LINE], tab[:, :], hot[:, :], start=True, stop=True).then_inc(sem("line_mm"), 1)
            for c in range(KD):
                if c == 0:
                    for t in range(NT):
                        pe.wait_ge(sem("x_normed"), t + 1)
                if c >= 2:
                    pe.wait_ge(sem("h_split"), c - 1)
                for t in range(NT):
                    mm = pe.transpose(bank[3 + c % 2][:, t * P:(t + 1) * P], x_tok[:, t, c * P:(c + 1) * P], ident)
                mm.then_inc(sem("x_T"), 1)

            pe.wait_ge(sem("h_split"), KD)
            run(gemm(stream.ba.at(0), hn_hi, hn_lo))
            run(gemm(stream.first.at(0), hn_hi, hn_lo), gemm(stream.first.at(1), hn_hi, hn_lo))
            pe.wait_ge(sem("ba_copied"), 1)
            for t in range(NT):
                mm = pe.transpose(bank[5][:, t * 16:t * 16 + 16], ba_sb[:, t * P:(t + 1) * P], ident[0:16, 0:16])
            mm.then_inc(sem("ba_T"), 1)
            pe.wait_ge(sem("slope_in"), 16)
            pe.wait_ge(sem("line_ready"), 1)
            for n in range(H // 2):
                if n >= 2:
                    pe.wait_ge(sem("bias_ready"), n - 1)
                pe.matmul(bank[6 + n % 2][:, :], flip, slope[:, 2 * n:2 * n + 2, :].rearrange("p a b -> p (a b)"),
                          start=True, stop=True).then_inc(sem("bias_mm"), 1)
            run(gemm(stream.first.at(2), hn_hi, hn_lo))
            pe.wait_ge(sem("g_ready"), 1)
            gg = gates[:, G_G, :, :].rearrange("p t h -> p (t h)")
            pe.matmul(bank[5][:, 64:96], cum, gg, start=True, stop=True)
            pe.matmul(bank[5][:, 96:128], half, gg, start=True, stop=True).then_inc(sem("g_sums"), 1)

            def qk_sum(h, n, c):
                pe.wait_ge(sem("a_sq"), h * 2 + (n + 1))
                pe.matmul(bank[c.bank][:, :], half, sqr[n][:, :], start=True, stop=True).then_inc(sem("a_sum"), 1)

            def v_turn(h, c):
                pe.wait_ge(bank_free[c.bank], c.uses + 1)
                for t in range(NT):
                    mm = pe.transpose(bank[7][:, t * P:(t + 1) * P], va_raw[:, t * P:(t + 1) * P], ident)
                mm.then_inc(sem("va_T"), 1)

            qk_sum(0, 0, stream.first.at(0))
            qk_sum(0, 1, stream.first.at(1))
            pe.wait_ge(sem("bias_ready"), H // 2)
            v_turn(0, stream.first.at(2))

            def scores(h, i):
                if i == 0:
                    pe.wait_ge(sem("qka_ready"), h * 2 + 3)
                if i == 1:
                    pe.wait_ge(sem("ob_done"), h + 1)
                if i >= 2:
                    pe.wait_ge(sem("a_exp"), h * 8 + (2 * i - 2) + 1)
                for j in range(2):
                    s = slice(64 * j, 64 * j + 64)
                    mm = pe.matmul(bank[3 + 2 * (i % 2) + j][:, 0:(i + 1) * P], qa[s, i * P:(i + 1) * P],
                                   ka[s, 0:(i + 1) * P], start=True, stop=True)
                mm.then_inc(sem("a_scores"), 1)

            def turn_w(h, i):
                pe.wait_ge(sem("a_w"), h * 4 + (i + 1))
                if i == 0:
                    pe.wait_ge(sem("va_ready"), h + 1)
                if i > 0:
                    pe.wait_ge(sem("a_wT"), h * 4 + i)
                for t in range(i + 1):
                    mm = pe.transpose(bank[7][:, t * P:(t + 1) * P], pr[0][:, t * P:(t + 1) * P], ident)
                mm.then_inc(sem("a_turned"), 1)

            def attend(h):
                pe.wait_ge(sem("a_wT"), h * 4 + 4)
                for t in range(NT):
                    mm = pe.matmul(bank[3][:, t * P:T], va[:, t * P:(t + 1) * P], wT[:, t, t * P:T],
                                   start=(t == 0), stop=(t == NT - 1), skip_group_check=True)
                mm.then_inc(sem("a_out"), 1)

            def head_a(h, seg):
                g = [gemm(seg.at(n, h) if seg is stream.heads else seg.at(n), hn_hi, hn_lo) for n in range(4)]
                scores(h, 0)
                scores(h, 1)
                run(g[0])
                turn_w(h, 0)
                scores(h, 2)
                run(g[1])
                turn_w(h, 1)
                scores(h, 3)
                run(g[2])
                turn_w(h, 2)
                f = Fill(g[3])
                f.step(4)
                turn_w(h, 3)
                f.rest()
                attend(h)

            def head_b(h, seg, fill):
                f = Fill(*fill)
                pe.wait_ge(sem("oa_sq"), h + 1)
                pe.matmul(bank[4][:, :], ones, sqr[0][:, :], start=True, stop=True).then_inc(sem("oa_sum"), 1)
                f.step(1)
                for n in range(2):
                    pe.wait_ge(sem("b_sq"), h * 2 + (n + 1))
                    pe.matmul(bank[5 + n][:, :], ones, sqb[n][:, :], start=True, stop=True).then_inc(sem("b_sum"), 1)
                pe.wait_ge(sem("g_cols"), h * 2 + 2)
                for t in range(NT):
                    mm = pe.matmul(tiles(7)[:, t, :], gcol[:, t, :], cum, start=True, stop=True)
                mm.then_inc(sem("g_rows"), 1)
                f.step(1)
                pe.wait_ge(sem("oa_done"), h + 2)
                for t in range(NT):
                    mm = pe.matmul(tiles(3)[:, t, :], bcol[:, t, :], ident, start=True, stop=True)
                mm.then_inc(sem("b_rows"), 1)
                f.step(1)
                pe.wait_ge(sem("qkb_ready"), h * 2 + 2)
                for t in range(NT):
                    s = slice(t * P, (t + 1) * P)
                    mm = pe.matmul(tiles(4)[:, t, :], kb[:, s], kb[:, s], start=True, stop=True)
                mm.then_inc(sem("kk"), 1)
                for t in range(NT):
                    s = slice(t * P, (t + 1) * P)
                    mm = pe.matmul(tiles(5)[:, t, :], kb[:, s], qb[:, s], start=True, stop=True)
                mm.then_inc(sem("qk"), 1)
                for t in range(NT):
                    mm = pe.transpose(tiles(6)[:, t, :], kb[:, t * P:(t + 1) * P], ident)
                mm.then_inc(sem("kb_T"), 1)
                pe.wait_ge(sem("g_rows_read"), h + 1)
                pe.wait_ge(sem("vb_ready"), h + 1)
                for t in range(NT):
                    mm = pe.transpose(tiles(7)[:, t, :], vb[:, t * P:(t + 1) * P], ident)
                mm.then_inc(sem("vb_T"), 1)
                f.step(1)
                pe.wait_ge(sem("ct"), h * 6 + 1)
                for t in range(NT):
                    mm = pe.matmul(tiles(3)[:, t, :], ct[0][:, t, :], ident, start=True, stop=True)
                mm.then_inc(sem("c1"), 1)
                f.step(2)
                for n in range(1, 6):
                    pe.wait_ge(sem("ct"), h * 6 + (n + 1))
                    pe.wait_ge(sem("xi"), h * 5 + n)
                    for t in range(NT):
                        mm = pe.matmul(tiles(4)[:, t, :], ct[n % 2][:, t, :], xi[:, t, :], start=True, stop=True)
                    mm.then_inc(sem("level_u"), 1)
                    f.step(1)
                    pe.wait_ge(sem("ui"), h * 5 + n)
                    pe.wait_ge(sem("xt"), h * 6 + n)
                    if n < 5:
                        for t in range(NT):
                            mm = pe.matmul(tiles(5)[:, t, :], xt[:, t, :], ui[:, t, :], start=True, stop=True)
                        mm.then_inc(sem("level_v"), 1)
                    for t in range(NT):
                        mm = pe.matmul(tiles(6)[:, t, :], ui[:, t, :], xt[:, t, :], start=True, stop=True)
                    mm.then_inc(sem("level_vt"), 1)
                    f.step(1)
                    if n == 3 and fill:
                        qk_sum(h + 1, 0, seg.at(4, h))
                pe.wait_ge(sem("xt"), h * 6 + 6)
                for t in range(NT):
                    mm = pe.matmul(tiles(7)[:, t, :], kbe[:, t, :], xt[:, t, :], start=True, stop=True)
                mm.then_inc(sem("w_mm"), 1)
                for t in range(NT):
                    mm = pe.matmul(tiles(3)[:, t, :], xt[:, t, :], vbt[:, t, :], start=True, stop=True)
                mm.then_inc(sem("u_mm"), 1)
                f.step(1)
                for c in range(NC):
                    t, r = c // 2, slice(64 * (c % 2), 64 * (c % 2) + 64)
                    cs = slice(c * CH, (c + 1) * CH)
                    if c == 0:
                        pe.wait_ge(sem("w_copied"), h + 1)
                    pe.wait_ge(sem("state"), h * 9 + (c + 1))
                    pe.matmul(bank[4][r, 0:P], wt_[:, t, r], state[:, :], start=True, stop=True).then_inc(sem("ws"), 1)
                    pe.matmul(bank[6][:, cs], state[:, :], qeg[:, t, r], start=True, stop=False, skip_group_check=True)
                    if c < 6:
                        f.step(1)
                    pe.wait_ge(sem("vnew"), h * 8 + (c + 1))
                    pe.matmul(bank[5][:, 0:P], kdec[r, t, :], vnew[r, :], start=True, stop=True).then_inc(sem("kv"), 1)
                    mm = pe.matmul(bank[6][:, cs], vnew[r, :], at_[r, t, r], start=False, stop=True, skip_group_check=True)
                    if c == 3 and fill:
                        qk_sum(h + 1, 1, seg.at(5, h))
                mm.then_inc(sem("ob_mm"), 1)
                f.rest()
                pe.wait_ge(sem("ob_sq"), h + 1)
                pe.matmul(bank[7][:, :], ones, sqb[0][:, :], start=True, stop=True).then_inc(sem("ob_sum"), 1)
                if fill:
                    pe.wait_ge(sem("ob_sum_read"), h + 1)
                    v_turn(h + 1, seg.at(6, h))

            with pe.Fori(0, H - 1) as h:
                head_a(h, stream.heads)
                head_b(h, stream.heads, [gemm(stream.heads.at(4 + n, h), hn_hi, hn_lo) for n in range(3)])
            head_a(H - 1, stream.last)
            head_b(H - 1, stream.last, [])

            pe.wait_ge(sem("ob_done"), H + 1)
            with pe.Fori(0, KD) as n:
                run(gemm(stream.mix.at(0, n), hn_hi, hn_lo))
                run(gemm(stream.mix.at(1, n), hn_hi, hn_lo))
                pe.wait_ge(sem("o_split"), 2)
                run(gemm(stream.mix.at(2, n), oa_hi, oa_lo))
                run(gemm(stream.mix.at(3, n), ob_hi, ob_lo))
            pe.wait_ge(sem("mix_sum"), KD + 1)
            pe.wait_ge(sem("x_back_in"), 16 * NT)
            for n in range(KD):
                c = stream.out.at(n % 4, n // 4)

                def residual(acc, n=n):
                    for t in range(NT):
                        mm = pe.matmul(acc[:, t * P:(t + 1) * P], x_back[:, t, n * P:(n + 1) * P], ident,
                                       start=False, stop=True, skip_group_check=True)
                    return mm
                run(gemm(c, mx_hi, mx_lo, more=residual))

            def norm_sum(stage):
                for c in range(KD):
                    pe.wait_ge(sem("n_sq"), stage * KD + c + 1)
                    pe.matmul(bank[4][:, :], ones, (u0, u1)[c % 2][:, :], start=(c == 0),
                              stop=(c == KD - 1)).then_inc(sem("n_sum"), 1)
                pe.wait_ge(sem("n_split"), (stage + 1) * KD)

            norm_sum(0)
            for name, part in FFN_ORDER:
                first_k, k = 8 * FFN_HALF[part], FFN_PARTS[part]
                if name == "up":
                    with pe.Fori(0, k // 2) as n:
                        for q in range(4):
                            run(gemm(stream.up[part].at(q, n), hn_hi, hn_lo))
                    if part == 0:
                        pe.wait_ge(sem("p_in"), 16)
                        for c in range(KP):
                            for t in range(NT):
                                mm = pe.transpose(tiles(5 + c)[:, t, :], p_tok[:, t, c * P:(c + 1) * P], ident)
                            mm.then_inc(sem("p_T"), 1)
                        pe.wait_ge(sem("p_split"), KP)
                else:
                    pe.wait_ge(sem("fa_lo"), FFN_FIRST[part] + k)
                    with pe.Fori(0, KD // 4) as n:
                        for q in range(4):
                            run(gemm(stream.down[part].at(q, n), fa_hi, fa_lo, k, first_k))
            norm_sum(1)
            def turn_y(c):
                pe.wait_ge(sem("yT"), c + 2)
                for t in range(NT):
                    mm = pe.transpose(tiles(5)[:, t, :], yT[:, t * P:(t + 1) * P], ident)
                mm.then_inc(sem("y_T"), 1)

            with pe.Fori(0, KD // 2) as n:
                for q in range(4):
                    if q % 2 == 0:
                        run(gemm(stream.ple.at(q, n), hn_hi, hn_lo))
                    else:
                        run(gemm(stream.ple.at(q, n), p_hi, p_lo, KP))
                        turn_y(2 * n + q // 2)

        @block.scalar
        def _(act):
            for name in ("a_exp",):
                act.sem_inc(sem(name), 1)
            def done(ins, name, value):
                ins.then_inc(sem(name) if isinstance(name, str) else name, 1)
                act.wait_ge(sem(name) if isinstance(name, str) else name, value)

            def rsqrt(dst, src, scale, names, value, eps=None):
                done(nc.scalar.activation(dst, src, ACT.Ln, bias=sm[:, 28:29], scale=scale), names[0], value)
                done(nc.scalar.activation(dst, dst, ACT.Exp, scale=-0.5), names[1], value)

            act.preload_act_table_set("natural_log_exp_and_others")
            act.wait_ge(sem("eps_set"), 1)
            for t in range(NT):
                act.wait_ge(sem(f"x_in{t}"), 16)
                done(nc.scalar.activation(junk[:, :], x_tok[:, t, :], ACT.Square, accum_out=ss0[:, t:t + 1]),
                     "x_sq", t + 1)
            done(nc.scalar.activation(lnx, ss0, ACT.Ln, bias=sm[:, 28:29], scale=1.0 / D), "x_ln", 1)
            done(nc.scalar.activation(rs0, lnx, ACT.Exp, scale=-0.5), "x_r", 1)
            act.wait_ge(sem("lam_sum"), 1)
            done(nc.scalar.activation(lam_s, lam_s, ACT.Exp), "lam_exp", 1)
            done(nc.scalar.activation(alexp, alog[:, :], ACT.Exp), "a_exp0", 1)
            act.wait_ge(sem("pt_ready"), 1)
            for c in range(KD):
                act.wait_ge(sem("x_T"), c + 1)
                done(nc.scalar.activation(hn_hi[:, c, :], bank[3 + c % 2][:, :], ACT.Copy,
                                          scale=pt[:, PA_ATTN + c:PA_ATTN + c + 1]), "h_high", c + 1)

            def prep_qk(h, n, c):
                dst = (qa_raw, ka_raw)[n]
                act.wait_ge(product_ready, c.number + 1)
                act.wait_ge(sem("qka_ready"), h * 2 + 1)
                act.wait_ge(sem("oa_done"), h + 1)
                done(nc.scalar.activation(dst[:, :], bank[c.bank][:, :], ACT.Copy), "qka_raw", h * 2 + (n + 1))
                done(nc.scalar.activation(sqr[n][:, :], dst[:, :], ACT.Square), "a_sq", h * 2 + (n + 1))

            def prep_r(h, n, c):
                act.wait_ge(sem("a_sum"), h * 2 + (n + 1))
                done(nc.scalar.activation(sqr[n][:, :], bank[c.bank][:, :], ACT.Ln, bias=sm[:, 28:29], scale=1.0 / 64),
                     bank_free[c.bank], c.uses + 1)
                done(nc.scalar.activation(sqr[n][:, :], sqr[n][:, :], ACT.Exp, scale=-0.5), "a_r", h * 2 + (n + 1))

            def prep_v(h, c):
                act.wait_ge(product_ready, c.number + 1)
                done(nc.scalar.activation(va_raw[:, :], bank[c.bank][:, :], ACT.Copy), bank_free[c.bank], c.uses + 1)

            def v_copy(h):
                act.wait_ge(sem("va_T"), h + 1)
                done(nc.scalar.activation(va[:, :], bank[7][:, :], ACT.Copy), "va_ready", h + 1)

            prep_qk(0, 0, stream.first.at(0))
            def plane(n):
                return gates[:, n, :, :].rearrange("p t h -> p (t h)")
            act.wait_ge(sem("ba_planes"), 2)
            done(nc.scalar.activation(plane(G_BETA), plane(G_B), ACT.Exp, scale=-1.0), "beta_exp", 1)
            done(nc.scalar.activation(plane(G_T), plane(G_A), ACT.Abs), "soft", 1)
            done(nc.scalar.activation(plane(G_U), plane(G_T), ACT.Exp, scale=-1.0), "soft", 2)
            done(nc.scalar.activation(plane(G_T), plane(G_U), ACT.Ln, bias=sm[:, 29:30]), "soft", 3)
            prep_qk(0, 1, stream.first.at(1))
            prep_v(0, stream.first.at(2))
            act.wait_ge(sem("g_cum"), 1)
            done(nc.scalar.activation(plane(G_EXP), plane(G_CUM), ACT.Exp), "g_exp", 1)
            act.wait_ge(sem("g_rest"), 1)
            done(nc.scalar.activation(plane(G_KD), plane(G_T), ACT.Exp), "g_kd", 1)
            prep_r(0, 0, stream.first.at(0))
            prep_r(0, 1, stream.first.at(1))
            v_copy(0)

            def softmax(h, i):
                w = (i + 1) * P
                act.wait_ge(sem("a_nmax"), h * 4 + (i + 1))
                act.wait_ge(sem("a_turned"), h * 4 + i + 1)
                for j in range(2):
                    done(nc.scalar.activation(pr[j][:, 0:w], bank[3 + 2 * (i % 2) + j][:, 0:w], ACT.Exp,
                                              bias=ast[:, 2 + j:3 + j], accum_out=ast[:, 4 + j:5 + j]),
                         "a_exp", h * 8 + (2 * i + j + 1) + 1)

            def keep_w(h, i):
                act.wait_ge(sem("a_turned"), h * 4 + (i + 1) + 1)
                done(nc.scalar.activation(wT[:, 0:i + 1, i * P:(i + 1) * P], tiles(7)[:, 0:i + 1, :], ACT.Copy),
                     "a_wT", h * 4 + (i + 1))

            def silu_exp(h, n, src=None):
                act.wait_ge(sem("b_conv"), h * 3 + (n + 1))
                done(nc.scalar.activation(silu[:, :], (qb, kb, vb)[n][:, :], ACT.Exp, scale=-1.0),
                     "b_exp", h * 3 + (n + 1))

            def square_b(h, n):
                act.wait_ge(sem("b_silu"), h * 2 + (n + 1))
                done(nc.scalar.activation(sqb[n][:, :], (qb, kb)[n][:, :], ACT.Square), "b_sq", h * 2 + (n + 1))

            def head_a(h, seg):
                def at(n):
                    return seg.at(n, h) if seg is stream.heads else seg.at(n)
                softmax(h, 0)
                softmax(h, 1)
                keep_w(h, 0)
                silu_exp(h, 0)
                softmax(h, 2)
                square_b(h, 0)
                silu_exp(h, 1)
                keep_w(h, 1)
                softmax(h, 3)
                square_b(h, 1)
                silu_exp(h, 2)
                keep_w(h, 2)
                keep_w(h, 3)
                c = at(3)
                act.wait_ge(product_ready, c.number + 1)
                act.wait_ge(sem("vb_ready"), h + 1)
                done(nc.scalar.activation(zb[:, :], bank[c.bank][:, :], ACT.Copy), "zb_raw", h + 1)
                done(nc.scalar.activation(silu[:, :], bank[c.bank][:, :], ACT.Exp, scale=-1.0), bank_free[c.bank], c.uses + 1)
                act.wait_ge(sem("a_out"), h + 1)
                done(nc.scalar.activation(sqr[0][:, :], bank[3][:, :], ACT.Square), "oa_sq", h + 1)

            def head_b(h, seg, more):
                act.wait_ge(sem("oa_sum"), h + 1)
                rsqrt(sqr[0][:, :], bank[4][:, :], 1.0 / P, ("oa_ln", "oa_r"), h + 1)
                for n in range(2):
                    act.wait_ge(sem("b_sum"), h * 2 + (n + 1))
                    rsqrt(sqb[n][:, :], bank[5 + n][:, :], 1.0, ("b_ln", "b_r"), h * 2 + (n + 1))
                act.wait_ge(sem("g_rows"), h + 1)
                done(nc.scalar.activation(eg[:, :, :].rearrange("p t c -> p (t c)"), bank[7][:, :], ACT.Exp), "eg", h + 1)
                act.wait_ge(sem("dec_arg"), h + 1)
                done(nc.scalar.activation(dec[:, :, :], dec[:, :, :], ACT.Exp), "dec", h + 1)
                for n in range(1, 6):
                    act.wait_ge(sem("level_u"), h * 5 + n)
                    done(nc.scalar.activation(ui[:, :, :], tiles(4), ACT.Copy), "ui", h * 5 + n)
                    if n == 3 and more:
                        prep_qk(h + 1, 0, seg.at(4, h))
                    if n == 4 and more:
                        prep_r(h + 1, 0, seg.at(4, h))
                act.wait_ge(sem("w_mm"), h + 1)
                done(nc.scalar.activation(wt_[:, :, :], tiles(7), ACT.Copy), "w_copied", h + 1)
                if more:
                    prep_qk(h + 1, 1, seg.at(5, h))
                    prep_r(h + 1, 1, seg.at(5, h))
                act.wait_ge(sem("ob_mm"), h + 1)
                done(nc.scalar.activation(sqb[0][:, :], bank[6][:, :], ACT.Square), "ob_sq", h + 1)
                if more:
                    prep_v(h + 1, seg.at(6, h))
                act.wait_ge(sem("ob_sum"), h + 1)
                rsqrt(sqb[0][:, :], bank[7][:, :], 1.0 / P, ("ob_sum_read", "ob_r"), h + 1)
                if more:
                    v_copy(h + 1)

            with act.Fori(0, H - 1) as h:
                head_a(h, stream.heads)
                head_b(h, stream.heads, True)
            head_a(H - 1, stream.last)
            head_b(H - 1, stream.last, False)

            act.wait_ge(sem("ob_done"), H + 1)
            done(nc.scalar.activation(oa_hi[:, :, :], o_a[:, :, :], ACT.Copy), "o_high", 1)
            done(nc.scalar.activation(ob_hi[:, :, :], o_b[:, :, :], ACT.Copy), "o_high", 2)
            with act.Fori(0, KD) as n:
                for q in range(2):
                    c = stream.mix.at(q, n)
                    act.wait_ge(product_ready, c.number + 1)
                    act.wait_ge(sem("mix_sum"), n + 1)
                    done(nc.scalar.activation(sg[q][:, :], bank[c.bank][:, :], ACT.Sigmoid), bank_free[c.bank], c.uses + 1)
            for n in range(KD):
                c = stream.out.at(n % 4, n // 4)
                act.wait_ge(product_ready, c.number + 1)
                done(nc.scalar.activation(x1[:, n, :], bank[c.bank][:, :], ACT.Copy), bank_free[c.bank], c.uses + 1)

            def norm(stage, gain):
                for c in range(KD):
                    if stage * KD + c >= 2:
                        act.wait_ge(sem("n_sum"), stage * KD + c - 1)
                    done(nc.scalar.activation((u0, u1)[c % 2][:, :], x1[:, c, :], ACT.Square), "n_sq", stage * KD + c + 1)
                act.wait_ge(sem("n_sum"), (stage + 1) * KD)
                rsqrt(rs[:, :], bank[4][:, :], 1.0 / D, ("n_ln", "n_r"), stage + 1)
                for c in range(KD):
                    act.wait_ge(sem("n_scaled"), stage * KD + c + 1)
                    done(nc.scalar.activation(hn_hi[:, c, :], (s0, tn)[c % 2][:, :], ACT.Copy,
                                              scale=pt[:, gain + c:gain + c + 1]), "n_high", stage * KD + c + 1)

            norm(0, PA_FFN)
            for name, part in FFN_ORDER:
                if name == "up":
                    with act.Fori(0, FFN_PARTS[part] // 2) as n:
                        for q in range(2):
                            act.wait_ge(sem("u_conv"), n * 2 + (FFN_FIRST[part] + q + 1))
                            done(nc.scalar.activation(s0[:, :], u0[:, :], ACT.Sigmoid), "u_sig",
                                 n * 2 + (FFN_FIRST[part] + q + 1))
                    if part == 0:
                        for c in range(KP):
                            act.wait_ge(sem("p_T"), c + 1)
                            done(nc.scalar.activation(p_hi[:, c, :], bank[5 + c][:, :], ACT.Copy), "p_high", c + 1)
            act.wait_ge(sem("x2_done"), 3 * KD)
            norm(1, PA_PLE)
            with act.Fori(0, KD // 2) as n:
                for q in range(2):
                    c = stream.ple.at(2 * q, n)
                    act.wait_ge(product_ready, c.number + 1)
                    act.wait_ge(sem("yT"), n * 2 + q + 1)
                    done(nc.scalar.activation(yg[:, :], bank[c.bank][:, :], ACT.Sigmoid), bank_free[c.bank], c.uses + 1)

        @block.vector
        def _(dve):
            for name in ("ob_done", "qka_ready", "oa_done", "mix_sum", "yT",):
                dve.sem_inc(sem(name), 1)
            dve.sem_inc(bank_free[3], 1)
            links = [0, 0, 0]

            def done(ins, name, value):
                ins.then_inc(sem(name) if isinstance(name, str) else name, 1)
                dve.wait_ge(sem(name) if isinstance(name, str) else name, value)

            def link(ins):
                links[2] += 1
                ins.then_inc(sem("vector_step"), 1)
                dve.wait_ge(sem("vector_step"), links[0] + links[2])

            def section():
                links[0], links[2] = links[0] + links[2], 0

            def loop(turns, body):
                section()
                base = links[0]
                per = count_links(body)
                with dve.Fori(0, turns) as i:
                    links[0], links[2] = i * per + base, 0
                    body(i)
                assert links[2] == per, (links, per)
                links[0], links[2] = base + per * turns, 0

            V = nc.vector

            done(V.memset(sm[:, 28:29], EPS), "eps_set0", 1)
            done(V.memset(sm[:, 29:30], 1.0), "eps_set", 1)
            done(V.memset(tab[32:33, :], NEG), "tab_set", 1)
            dve.wait_ge(sem("params_in"), 16 * 13)
            dve.wait_ge(sem("small_in"), 16 * 5)
            link(V.tensor_tensor(lamp[:, :, :], lamr[:, 0:4:2, :], lamr[:, 1:4:2, :], ALU.mult))
            done(V.tensor_reduce(lam_s, lamp[:, :, :], AX_X, ALU.add), "lam_sum", 1)
            dve.wait_ge(sem("x_r"), 1)
            for t in range(NT):
                done(V.tensor_scalar(x_tok[:, t, :], x_tok[:, t, :], rs0[:, t:t + 1], None, ALU.mult), "x_normed", t + 1)
            dve.wait_ge(sem("params_T"), 1)
            link(V.tensor_copy(pt[:, 0:124], bank[7][:, 0:124]))
            link(V.tensor_copy(pt[:, P:P + 88], bank[7][:, P:P + 88]))
            done(V.tensor_copy(pt[:, 2 * P:2 * P + 88], bank[7][:, 2 * P:2 * P + 88]), "pt_ready", 1)
            dve.wait_ge(sem("line_mm"), 1)
            done(V.tensor_copy(line[:, :], bank[6][0:H, 0:LINE]), "line_ready", 1)
            for c in range(KD):
                dve.wait_ge(sem("h_high"), c + 1)
                done(V.scalar_tensor_tensor(out=hn_lo[:, c, :], in0=bank[3 + c % 2][:, :],
                                            scalar=pt[:, PA_ATTN + c:PA_ATTN + c + 1],
                                            in1=hn_hi[:, c, :].bitcast(F32), op0=ALU.mult, op1=ALU.subtract),
                     "h_split", c + 1)
            dve.wait_ge(sem("lam_exp"), 1)
            link(V.tensor_scalar(nlam, lam_s[:, 1:2], lam_s[:, 0:1], -LAM_INIT, ALU.subtract, ALU.add))
            link(V.tensor_scalar(gq8, pt[:, PA_QN:PA_QN + 1], 64 ** -0.5, None, ALU.mult))
            link(V.tensor_scalar(gsub, pt[:, PA_SUB:PA_SUB + 1], 1.0 - LAM_INIT, None, ALU.mult))
            c = stream.ba.at(0)
            dve.wait_ge(product_ready, c.number + 1)
            link(V.tensor_copy(ba_sb[:, :], bank[c.bank][0:16, :]))
            done(V.tensor_copy(ba_sb[:, 0:1], ba_sb[:, 0:1]), "ba_copied", 1)
            dve.sem_inc(bank_free[c.bank], 1)
            dve.wait_ge(sem("ba_T"), 1)
            turned = bank[5][:, 0:64].rearrange("p (t c) -> p t c", c=16)
            done(V.tensor_copy(gt(G_B), turned[:, :, 0:H]), "ba_planes", 1)
            dve.wait_ge(sem("a_exp0"), 1)
            done(V.tensor_tensor(gt(G_A), turned[:, :, H:2 * H],
                                 dtb[:, :].unsqueeze(1).to_broadcast([P, NT, H]), ALU.add), "ba_planes", 2)
            for n in range(H // 2):
                dve.wait_ge(sem("bias_mm"), n + 1)
                done(V.tensor_copy(bias[:, 2 * n:2 * n + 2, :].rearrange("p a b -> p (a b)"), bank[6 + n % 2][:, :]),
                     "bias_ready", n + 1)
            dve.wait_ge(sem("soft"), 3)
            link(V.tensor_scalar(gt(G_BETA), gt(G_BETA), 1.0, None, ALU.add))
            link(V.reciprocal(gt(G_BETA), gt(G_BETA)))
            link(V.scalar_tensor_tensor(out=gt(G_U), in0=gt(G_A), scalar=0.0, in1=gt(G_T), op0=ALU.max, op1=ALU.add))
            done(V.scalar_tensor_tensor(out=gt(G_G), in0=gt(G_U), scalar=-1.0,
                                        in1=alexp.unsqueeze(1).to_broadcast([P, NT, H]), op0=ALU.mult, op1=ALU.mult),
                 "g_ready", 1)
            dve.wait_ge(sem("g_sums"), 1)
            done(V.tensor_copy(gates[:, G_CUM, :, :].rearrange("p t h -> p (t h)"), bank[5][:, 64:96]), "g_cum", 1)
            done(V.tensor_tensor(gates[:, G_T, :, :].rearrange("p t h -> p (t h)"), bank[5][:, 96:128],
                                 gates[:, G_CUM, :, :].rearrange("p t h -> p (t h)"), ALU.subtract), "g_rest", 1)
            dve.wait_ge(sem("g_kd"), 1)
            link(V.tensor_tensor(gt(G_BEG), gt(G_BETA), gt(G_EXP), ALU.mult))

            def prep(h, n):
                dve.wait_ge(sem("a_r"), h * 2 + (n + 1))
                dve.wait_ge(sem("a_scores"), h * 4 + 1)
                done(V.scalar_tensor_tensor(out=(qa, ka)[n][:, :], in0=(qa_raw, ka_raw)[n][:, :],
                                            scalar=(gq8, pt[:, PA_KN:PA_KN + 1])[n], in1=sqr[n][:, :],
                                            op0=ALU.mult, op1=ALU.mult), "qka_ready", h * 2 + (n + 1) + 1)

            def maxima(h, i):
                w, near = (i + 1) * P, min(i + 1, 2) * P
                both = pairs(i)
                dve.wait_ge(sem("a_scores"), h * 4 + (i + 1) + 1)
                for j in range(2):
                    b = bank[3 + 2 * (i % 2) + j]
                    link(V.tensor_tensor(b[:, w - near:w], b[:, w - near:w], bias_of(h, near), ALU.add))
                dve.wait_ge(sem("a_exp"), h * 8 + 2 * i + 1)
                for j in range(2):
                    link(V.tensor_reduce(ast[:, j:j + 1], bank[3 + 2 * (i % 2) + j][:, 0:w], AX_X, ALU.max))
                done(V.tensor_scalar(ast[:, 2:4], ast[:, 0:2], -1.0, None, ALU.mult), "a_nmax", h * 4 + (i + 1))

            def pairs(i):
                return None

            def bias_of(h, near):
                return bias[:, bass.ds(h, 1), 256 - near:256].rearrange("p a b -> p (a b)")

            def combine(h, i):
                w = (i + 1) * P
                dve.wait_ge(sem("a_exp"), h * 8 + (2 * i + 2) + 1)
                link(V.reciprocal(ast[:, 6:8], ast[:, 4:6]))
                link(V.tensor_scalar(ast[:, 8:9], ast[:, 7:8], nlam, None, ALU.mult))
                link(V.tensor_scalar(pr[1][:, 0:w], pr[1][:, 0:w], ast[:, 8:9], None, ALU.mult))
                done(V.scalar_tensor_tensor(out=pr[0][:, 0:w], in0=pr[0][:, 0:w], scalar=ast[:, 6:7],
                                            in1=pr[1][:, 0:w], op0=ALU.mult, op1=ALU.add), "a_w", h * 4 + (i + 1))

            def conv(h, n, c):
                y, src = (qb, kb, vb)[n], bank[c.bank]
                dve.wait_ge(product_ready, c.number + 1)
                dve.wait_ge(sem("ob_done"), h + 1)

                def tap(j):
                    return col(PA_CONV + 24 * j + 8 * n, h)
                link(V.tensor_scalar(y[:, :], src[:, :], tap(3), None, ALU.mult))
                for j, back in ((2, 1), (1, 2)):
                    link(V.scalar_tensor_tensor(out=y[:, back:], in0=src[:, 0:T - back], scalar=tap(j),
                                                in1=y[:, back:], op0=ALU.mult, op1=ALU.add))
                done(V.scalar_tensor_tensor(out=y[:, 3:], in0=src[:, 0:T - 3], scalar=tap(0),
                                            in1=y[:, 3:], op0=ALU.mult, op1=ALU.add), bank_free[c.bank], c.uses + 1)
                dve.sem_inc(sem("b_conv"), 1)

            def finish_silu(h, n):
                dve.wait_ge(sem("b_exp"), h * 3 + (n + 1))
                link(V.tensor_scalar(silu[:, :], silu[:, :], 1.0, None, ALU.add))
                link(V.reciprocal(silu[:, :], silu[:, :]))
                y = (qb, kb, vb)[n]
                done(V.tensor_tensor(y[:, :], y[:, :], silu[:, :], ALU.mult), *(
                    ("b_silu", h * 2 + (n + 1)) if n < 2 else ("vb_ready", h + 1)))

            def flat(t):
                return t[:, :, :].rearrange("p t c -> p (t c)")

            def head_a(h, seg):
                def at(n):
                    return seg.at(n, h) if seg is stream.heads else seg.at(n)
                maxima(h, 0)
                maxima(h, 1)
                combine(h, 0)
                conv(h, 0, at(0))
                maxima(h, 2)
                finish_silu(h, 0)
                combine(h, 1)
                conv(h, 1, at(1))
                maxima(h, 3)
                finish_silu(h, 1)
                combine(h, 2)
                conv(h, 2, at(2))
                combine(h, 3)
                finish_silu(h, 2)
                c = at(3)
                dve.wait_ge(bank_free[c.bank], c.uses + 1)
                link(V.tensor_scalar(silu[:, :], silu[:, :], 1.0, None, ALU.add))
                link(V.reciprocal(silu[:, :], silu[:, :]))
                link(V.tensor_tensor(zb[:, :], zb[:, :], silu[:, :], ALU.mult))
                for n, (dst, g) in enumerate(((gcol, G_G), (bcol, G_BETA))):
                    done(V.tensor_scalar(dst[:, :, :], gcols(g, h).to_broadcast([P, NT, P]), 1.0, None, ALU.mult),
                         "g_cols", h * 2 + (n + 1))

            def level_mask(n):
                return const(C_LEVEL + n).unsqueeze(1).to_broadcast([P, NT, P])

            def make_ct(h, n):
                done(V.tensor_tensor(ct[n % 2][:, :, :], lt[:, :, :], level_mask(n), ALU.mult), "ct", h * 6 + (n + 1))

            def head_b(h, seg, more):
                dve.wait_ge(sem("oa_r"), h + 1)
                done(V.scalar_tensor_tensor(out=dyn(o_a, h), in0=bank[3][:, :], scalar=gsub, in1=sqr[0][:, :],
                                            op0=ALU.mult, op1=ALU.mult), "oa_done", h + 2)
                for n, scale in ((0, P ** -0.5), (1, 1.0)):
                    dve.wait_ge(sem("b_r"), h * 2 + (n + 1))
                    y = (qb, kb)[n]
                    done(V.scalar_tensor_tensor(out=y[:, :], in0=y[:, :], scalar=scale, in1=sqb[n][:, :],
                                                op0=ALU.mult, op1=ALU.mult), "qkb_ready", h * 2 + (n + 1))
                dve.wait_ge(sem("eg"), h + 1)
                for t in range(NT):
                    ins = V.scalar_tensor_tensor(out=dec[:, t, :], in0=tiles(7)[:, t, :],
                                                 scalar=gates[:, G_CUM, t, bass.ds(h, 1)], in1=mask,
                                                 op0=ALU.subtract, op1=ALU.add)
                    if t < NT - 1:
                        link(ins)
                    else:
                        done(ins, "g_rows_read", h + 1)
                        dve.sem_inc(sem("dec_arg"), 1)
                link(V.tensor_tensor(flat(qeg), qb[:, :], flat(eg), ALU.mult))
                dve.wait_ge(sem("dec"), h + 1)
                dve.wait_ge(sem("b_rows"), h + 1)
                link(V.tensor_tensor(flat(decb), flat(dec), bank[3][:, :], ALU.mult))
                dve.wait_ge(sem("kk"), h + 1)
                link(V.tensor_tensor(flat(lt), bank[4][:, :], flat(decb), ALU.mult))
                make_ct(h, 0)
                done(V.tensor_tensor(xt[:, :, :], ident.unsqueeze(1).to_broadcast([P, NT, P]), ct[0][:, :, :],
                                     ALU.subtract), "xt", h * 6 + 1)
                make_ct(h, 1)
                dve.wait_ge(sem("qk"), h + 1)
                link(V.tensor_tensor(flat(at_), bank[5][:, :], flat(dec), ALU.mult))
                dve.wait_ge(sem("kb_T"), h + 1)
                link(V.tensor_tensor(kbe[:, :, :], tiles(6), gcols(G_BEG, h).to_broadcast([P, NT, P]), ALU.mult))
                link(V.tensor_tensor(kdec[:, :, :], tiles(6), gcols(G_KD, h).to_broadcast([P, NT, P]), ALU.mult))
                dve.wait_ge(sem("vb_T"), h + 1)
                link(V.tensor_tensor(vbt[:, :, :], tiles(7), gcols(G_BETA, h).to_broadcast([P, NT, P]), ALU.mult))
                dve.wait_ge(sem("c1"), h + 1)
                done(V.tensor_tensor(xi[:, :, :], ident.unsqueeze(1).to_broadcast([P, NT, P]), tiles(3),
                                     ALU.subtract), "xi", h * 5 + 1)
                for n in range(1, 6):
                    if n < 5:
                        make_ct(h, n + 1)
                        dve.wait_ge(sem("level_v"), h * 4 + n)
                        done(V.tensor_tensor(xi[:, :, :], xi[:, :, :], tiles(5), ALU.subtract), "xi", h * 5 + (n + 1))
                    dve.wait_ge(sem("level_vt"), h * 5 + n)
                    done(V.tensor_tensor(xt[:, :, :], xt[:, :, :], tiles(6), ALU.subtract), "xt", h * 6 + (n + 1))
                    if n == 5 and more:
                        prep(h + 1, 0)
                done(V.memset(state[:, :], 0.0), "state", h * 9 + 1)
                dve.wait_ge(sem("u_mm"), h + 1)
                link(V.tensor_copy(flat(us), bank[3][:, :]))
                for c in range(NC):
                    t, r = c // 2, slice(64 * (c % 2), 64 * (c % 2) + 64)
                    dve.wait_ge(sem("ws"), h * 8 + (c + 1))
                    done(V.tensor_tensor(vnew[r, :], us[r, t, :], bank[4][r, 0:P], ALU.subtract), "vnew", h * 8 + (c + 1))
                    dve.wait_ge(sem("kv"), h * 8 + (c + 1))
                    last = 64 * (c % 2) + 63
                    done(V.scalar_tensor_tensor(out=state[:, :], in0=state[:, :], scalar=eg[:, t, last:last + 1],
                                                in1=bank[5][:, 0:P], op0=ALU.mult, op1=ALU.add),
                         "state", h * 9 + (c + 2))
                    if c == 5 and more:
                        prep(h + 1, 1)
                dve.wait_ge(sem("ob_r"), h + 1)
                link(V.scalar_tensor_tensor(out=silu[:, :], in0=bank[6][:, :], scalar=col(PA_ON), in1=sqb[0][:, :],
                                            op0=ALU.mult, op1=ALU.mult))
                done(V.tensor_tensor(dyn(o_b, h), silu[:, :], zb[:, :], ALU.mult), "ob_done", h + 2)

            def count_links(body):
                return LINKS[body]

            def head_turn(h):
                head_a(h, stream.heads)
                head_b(h, stream.heads, True)

            prep(0, 0)
            prep(0, 1)
            LINKS = {head_turn: 58}
            loop(H - 1, head_turn)
            head_a(H - 1, stream.last)
            head_b(H - 1, stream.last, False)

            for n, (hi, lo, o) in enumerate(((oa_hi, oa_lo, o_a), (ob_hi, ob_lo, o_b))):
                dve.wait_ge(sem("o_high"), n + 1)
                done(V.tensor_tensor(lo[:, :, :], o[:, :, :], hi[:, :, :].bitcast(F32), ALU.subtract), "o_split", n + 1)

            def mix_turn(n):
                for q in range(2):
                    c = stream.mix.at(2 + q, n)
                    dve.wait_ge(product_ready, c.number + 1)
                    dve.wait_ge(bank_free[q], stream.mix.at(q, n).uses + 1)
                    done(V.tensor_tensor(sg[q][:, :], sg[q][:, :], bank[c.bank][:, :], ALU.mult), bank_free[c.bank], c.uses + 1)
                link(V.tensor_tensor(sg[0][:, :], sg[0][:, :], sg[1][:, :], ALU.add))
                link(V.tensor_scalar(dyn(mx_hi, n), sg[0][:, :], 1.0, None, ALU.mult))
                link(V.tensor_tensor(dyn(mx_lo, n), sg[0][:, :], dyn(mx_hi, n).bitcast(F32), ALU.subtract))
                dve.sem_inc(sem("mix_sum"), 1)

            LINKS[mix_turn] = 3
            loop(KD, mix_turn)

            def norm(stage, gain):
                dve.wait_ge(sem("n_r"), stage + 1)
                dve.wait_ge(product_ready, (stream.up[0].first, stream.ple.first)[stage])

                def scaled(c):
                    done(V.tensor_tensor((s0, tn)[c % 2][:, :], x1[:, c, :], rs[:, :], ALU.mult), "n_scaled",
                         stage * KD + c + 1)
                scaled(0)
                for c in range(KD):
                    if c < KD - 1:
                        scaled(c + 1)
                    dve.wait_ge(sem("n_high"), stage * KD + c + 1)
                    done(V.scalar_tensor_tensor(out=hn_lo[:, c, :], in0=(s0, tn)[c % 2][:, :],
                                                scalar=pt[:, gain + c:gain + c + 1],
                                                in1=hn_hi[:, c, :].bitcast(F32), op0=ALU.mult, op1=ALU.subtract),
                         "n_split", stage * KD + c + 1)

            norm(0, PA_FFN)

            def up_turn(part):
                def body(n):
                    for pair in range(2):
                        f = n * 2 + (FFN_FIRST[part] + pair)
                        for q, u in ((0, u0), (1, u1)):
                            c = stream.up[part].at(2 * pair + q, n)
                            src = bank[c.bank]

                            def tap(j):
                                return col(PA_TAP[j] + q * KF, f)
                            dve.wait_ge(product_ready, c.number + 1)
                            link(V.tensor_scalar(u[:, :], src[:, :], tap(2), col(PA_FBIAS + q * KF, f), ALU.mult, ALU.add))
                            link(V.scalar_tensor_tensor(out=u[:, 1:], in0=src[:, 0:T - 1], scalar=tap(1), in1=u[:, 1:],
                                                        op0=ALU.mult, op1=ALU.add))
                            done(V.scalar_tensor_tensor(out=u[:, 2:], in0=src[:, 0:T - 2], scalar=tap(0), in1=u[:, 2:],
                                                        op0=ALU.mult, op1=ALU.add), bank_free[c.bank], c.uses + 1)
                            if q == 0:
                                dve.sem_inc(sem("u_conv"), 1)
                        dve.wait_ge(sem("u_sig"), f + 1)
                        link(V.tensor_tensor(tn[:, :], u0[:, :], s0[:, :], ALU.mult))
                        link(V.tensor_tensor(tn[:, :], tn[:, :], u1[:, :], ALU.mult))
                        k = n * 2 + (8 * FFN_HALF[part] + pair)
                        link(V.tensor_scalar(dyn(fa_hi, k), tn[:, :], 1.0, None, ALU.mult))
                        done(V.tensor_tensor(dyn(fa_lo, k), tn[:, :], dyn(fa_hi, k).bitcast(F32), ALU.subtract),
                             "fa_lo", f + 1)
                LINKS[body] = 14
                return body

            downs = 0
            for name, part in FFN_ORDER:
                if name == "up":
                    if part == 2:
                        dve.wait_ge(product_ready, stream.up[2].first)
                    loop(FFN_PARTS[part] // 2, up_turn(part))
                    if part == 0:
                        for c in range(KP):
                            dve.wait_ge(sem("p_high"), c + 1)
                            done(V.tensor_tensor(p_lo[:, c, :], bank[5 + c][:, :], p_hi[:, c, :].bitcast(F32), ALU.subtract),
                                 "p_split", c + 1)
                else:
                    def down_turn(n, part=part, downs=downs):
                        for q in range(4):
                            c = stream.down[part].at(q, n)
                            dve.wait_ge(product_ready, c.number + 1)
                            k = n * 4 + q
                            link(V.tensor_tensor(dyn(x1, k), dyn(x1, k), bank[c.bank][:, :], ALU.add))
                            dve.sem_inc(bank_free[c.bank], 1)
                            dve.sem_inc(sem("x2_done"), 1)
                    LINKS[down_turn] = 4
                    loop(KD // 4, down_turn)
                    downs += 1
            norm(1, PA_PLE)

            def ple_turn(n):
                for q in range(2):
                    k = n * 2 + q
                    g, c = stream.ple.at(2 * q, n), stream.ple.at(2 * q + 1, n)
                    dve.wait_ge(bank_free[g.bank], g.uses + 1)
                    dve.wait_ge(product_ready, c.number + 1)
                    done(V.tensor_tensor(yT[:, :], yg[:, :], bank[c.bank][:, :], ALU.mult), bank_free[c.bank], c.uses + 1)
                    done(V.tensor_tensor(yT[:, :], yT[:, :], dyn(x1, k), ALU.add), "yT", k + 2)
                    dve.wait_ge(sem("y_T"), k + 1)
                    done(V.tensor_scalar(y_tok[:, :, bass.ds(k * P, P)], tiles(5), 1.0, None, ALU.mult), "y_ready", k + 1)

            LINKS[ple_turn] = 0
            loop(KD // 2, ple_turn)


_INS = ["x", "p", "w_in", "attn_norm", "qnorm_a", "knorm_a", "lam_a", "subln_a", "rel_bias", "conv_b",
        "a_log_b", "dt_bias_b", "onorm_b", "w_br_a", "w_br_b", "w_out", "ffn_norm", "w_up", "conv_ff",
        "conv_ff_bias", "w_down", "ple_norm", "w_ple_gate", "w_ple_proj"]


def kernel(**inputs):
    import concourse.bacc as bacc
    from concourse.bass_utils import run_bass_kernel_spmd

    nc = bacc.Bacc("TRN2", target_bir_lowering=False, num_devices=1)
    arrays = {f"in_{name}": np.ascontiguousarray(inputs[name]) for name in _INS}
    arrays["in_consts"] = constants()
    args = [nc.dram_tensor(n, a.shape, mybir.dt.from_np(a.dtype), kind="ExternalInput").ap()
            for n, a in arrays.items()]
    args.append(nc.dram_tensor("out_0", (1, T, D), F32, kind="ExternalOutput").ap())
    build(nc, *args)
    r = run_bass_kernel_spmd(nc, [arrays], core_ids=[0])
    return r.results[0]["out_0"]
```

```python
import math
from contextlib import ExitStack

import numpy as np

import concourse.bass as bass
from concourse import mybir

F32 = mybir.dt.float32
F32R = mybir.dt.float32r
ALU = mybir.AluOpType
ACT = mybir.ActivationFunctionType
AX_X = mybir.AxisListType.X

P = 128
T = 512
NT = T // P
D = 1024
KD = D // P
H = 8
CH = 64
NC = T // CH
LEVELS = (1, 2, 4, 8, 16, 32)
FF = 2816
KF = FF // P
PLE = 256
KP = PLE // P
EPS = 1e-6
NEG = -1e30
LAM_INIT = 0.8 - 0.6 * math.exp(0.0)
COLS = {"qa": 0, "ka": D, "va": 2 * D, "qb": 3 * D, "kb": 4 * D, "vb": 5 * D, "zb": 6 * D,
        "ba": 7 * D, "g0": 7 * D + 16, "g1": 8 * D + 16}

C_ID, C_FLIP, C_CUM, C_HALF, C_ONES, C_MASK, C_LEVEL, C_HOT = 0, 1, 2, 3, 4, 5, 6, 12
CONST_COLS = C_HOT * P + 384
LINE = 384

PA_ATTN, PA_FFN, PA_PLE, PA_CONV, PA_QN, PA_KN, PA_SUB, PA_ON = 0, 8, 16, 24, 120, 121, 122, 123
PA_TAP = (128, 128 + 44, 256)
PA_FBIAS = 256 + 44


def constants():
    c = np.zeros((P, CONST_COLS), np.float32)
    j, i = np.meshgrid(np.arange(P), np.arange(P), indexing="ij")
    same = (j // CH) == (i // CH)

    def put(n, a):
        c[:, n * P:(n + 1) * P] = a

    put(C_ID, j == i)
    put(C_FLIP, j + i == P - 1)
    put(C_CUM, same & (j <= i))
    put(C_HALF, same)
    put(C_ONES, np.ones((P, P)))
    put(C_MASK, np.where(same & (j <= i), 0.0, NEG))
    for n, m in enumerate(LEVELS):
        put(C_LEVEL + n, (j // (2 * m) == i // (2 * m)) & (j // m % 2 == 0) & (i // m % 2 == 1))
    r = 255 - np.arange(LINE)
    n = np.maximum(r, 0)
    big = 16 + (np.log(np.maximum(n, 1) / 16) / math.log(128 / 16) * 16).astype(np.int64)
    bucket = np.where(n < 16, n, np.minimum(big, 31))
    hot = np.zeros((33, LINE), np.float32)
    hot[np.where(r >= 0, bucket, 32), np.arange(LINE)] = 1.0
    hot[31] -= 1.0
    c[0:33, C_HOT * P:] = hot
    return c


class Chunk:

    def __init__(self, number, slot, arrival, bank, uses):
        self.number = number
        self.slot = slot
        self.arrival = arrival
        self.bank = bank
        self.uses = uses


class Segment:

    def __init__(self, stream, turns, slots, banks):
        self.first, self.turns, self.slots, self.banks = stream.count, turns, slots, banks
        self.slot0, self.bank0 = dict(stream.slot), dict(stream.bank)
        stream.count += turns * len(slots)
        for s in slots:
            stream.slot[s] = stream.slot.get(s, 0) + turns
        for b in banks:
            stream.bank[b] = stream.bank.get(b, 0) + turns

    def at(self, n, turn=0):
        turn, n = turn + n // len(self.slots), n % len(self.slots)
        s, b = self.slots[n], self.banks[n]
        return Chunk(turn * len(self.slots) + (self.first + n), s,
                     turn * self.slots.count(s) + (self.slot0.get(s, 0) + self.slots[:n].count(s) + 1),
                     b, turn * self.banks.count(b) + (self.bank0.get(b, 0) + self.banks[:n].count(b)))


TURN = ("qa", "ka", "zb", "qb", "kb", "vb", "va")
LEAD = ("qa", "ka", "qb", "kb", "vb", "va")
LATE = ("zb", "qb", "kb", "vb")
LAST = ("zb",)
AHEAD = {"qa": 2, "ka": 2, "va": 2, "qb": 1, "kb": 1, "vb": 1, "zb": 0}


class Stream:

    def __init__(self):
        self.count, self.slot, self.bank = 0, {}, {3: 1}
        self.ba = Segment(self, 1, [0], [0])
        self.first = Segment(self, 1, [1, 2, 3], [1, 0, 2])
        self.lead = Segment(self, 1, [0, 1, 2, 3, 0, 1], [1, 0, 2, 1, 2, 0])
        self.heads = Segment(self, H - 2, [2, 3, 0, 1, 2, 0, 1], [1, 0, 2, 1, 0, 2, 1])
        self.late = Segment(self, 1, [2, 3, 0, 1], [0, 1, 2, 0])
        self.last = Segment(self, 1, [2], [2])
        slots, four = [3, 0, 1, 2], [0, 1, 2, 3]
        self.mix_a = Segment(self, KD // 2, slots, [1, 0, 2, 3])
        self.mix_b = Segment(self, KD // 2, slots, four)
        self.out = Segment(self, KD // 4, slots, four)
        self.up = [None] * 3
        self.down = [None] * 3
        for name, n in FFN_ORDER:
            if name == "up":
                self.up[n] = Segment(self, FFN_PARTS[n] // 2, slots, four)
            else:
                self.down[n] = Segment(self, KD // 4, slots, four)
        self.ple = Segment(self, KD // 2, slots, four)


FFN_PARTS = (8, 8, 6)
FFN_FIRST = (0, 8, 16)
FFN_ORDER = (("up", 0), ("up", 1), ("down", 0), ("up", 2), ("down", 1), ("down", 2))
FFN_HALF = (0, 1, 0)


def build(nc, x, p, w_in, attn_norm, qnorm_a, knorm_a, lam_a, subln_a, rel_bias, conv_b, a_log_b,
          dt_bias_b, onorm_b, w_br_a, w_br_b, w_out, ffn_norm, w_up, conv_ff, conv_ff_bias, w_down,
          ple_norm, w_ple_gate, w_ple_proj, consts, out):
    stream = Stream()
    ctx = ExitStack()
    with ctx:
        def sb(name, shape, dt=F32, stack=ctx):
            return stack.enter_context(nc.sbuf_tensor(name, shape, dt))

        sems = {}

        def sem(name):
            if name not in sems:
                sems[name] = ctx.enter_context(nc.semaphore(name))
            return sems[name]

        raw = [sb(f"w_raw{s}", [P, KD, P]) for s in range(4)]
        whi = [sb(f"w_hi{s}", [P, KD, P], F32R) for s in range(4)]
        wlo = [sb(f"w_lo{s}", [P, KD, P], F32R) for s in range(4)]
        hn_hi = sb("hn_hi", [P, KD, T], F32R)
        hn_lo = sb("hn_lo", [P, KD, T], F32R)
        sq = sb("sq", [P, C_HOT * P])
        pt = sb("pt", [P, 3 * P])
        sm = sb("sm", [P, 64])


        def const(n):
            return sq[:, n * P:(n + 1) * P]

        ident, flip, cum, half, ones, mask = map(const, range(6))

        room = ExitStack()
        mx_hi = sb("mx_hi", [P, KD, T], F32R, room)
        mx_lo = sb("mx_lo", [P, KD, T], F32R, room)
        room.close()
        room = ExitStack()
        u0, u1, s0, tn, vr = (sb(n, [P, T], F32, room) for n in ("u0", "u1", "s0", "tn", "vr"))
        p_tok = sb("p_tok", [P, NT, PLE], F32, room)
        p_hi = sb("p_hi", [P, KP, T], F32R, room)
        p_lo = sb("p_lo", [P, KP, T], F32R, room)
        room.close()
        o_a = sb("o_a", [P, H, T])
        o_b = sb("o_b", [P, H, T])
        ws = ExitStack()
        bias = sb("bias", [P, H, 256], F32, ws)
        qa_raw, ka_raw, va_raw, qa, ka, va = (
            sb(n, [P, T], F32, ws) for n in ("qa_raw", "ka_raw", "va_raw", "qa", "ka", "va"))
        pr = [sb(f"pr{j}", [P, T], F32, ws) for j in range(2)]
        wT = sb("wT", [P, NT, T], F32, ws)
        gates = sb("gates", [P, 12, NT, H], F32, ws)
        sqr = [sb(f"sqr{n}", [P, T], F32, ws) for n in range(2)]
        first = ExitStack()
        x_tok = sb("x_tok", [P, NT, D], F32, first)
        prow = sb("prow", [P, 3, P], F32, first)
        hot = sb("hot", [33, LINE], F32, first)
        tab = sb("tab", [33, H], F32, first)
        line = sb("line", [H, LINE], F32, first)
        slope = sb("slope", [P, H, 256], F32, first)
        lamr = sb("lamr", [P, 4, 64], F32, first)
        lamp = sb("lamp", [P, 2, 64], F32, first)
        ba_sb = sb("ba_sb", [16, T], F32, first)
        junk = sb("junk", [P, D], F32, first)
        alog = sb("alog", [P, H], F32, first)
        dtb = sb("dtb", [P, H], F32, first)
        first.close()
        qb, kb, vb, zb = (sb(n, [P, T], F32, ws) for n in ("qb", "kb", "vb", "zb"))
        silu = sb("silu", [P, T], F32, ws)
        sqb = [sb(f"sqb{n}", [P, T], F32, ws) for n in range(2)]
        sqo = sb("sqo", [P, T], F32, ws)
        gcol, bcol = sb("gcol", [P, NT, P], F32, ws), sb("bcol", [P, NT, P], F32, ws)
        qeg, eg, dec, decb, lt, at_ = (
            sb(n, [P, NT, P], F32, ws) for n in ("qeg", "eg", "dec", "decb", "lt", "at_"))
        ct = [sb(f"ct{n}", [P, NT, P], F32, ws) for n in range(2)]
        xi, xt, ui = (sb(n, [P, NT, P], F32, ws) for n in ("xi", "xt", "ui"))
        vbt, kbe, kdec = (sb(n, [P, NT, P], F32, ws) for n in ("vbt", "kbe", "kdec"))
        state, vnew = sb("state", [P, P], F32, ws), sb("vnew", [P, P], F32, ws)
        ast = sb("ast", [P, 16], F32, ws)
        wt_, us = ui, vbt
        ws.close()
        ws = ExitStack()
        oa_hi, oa_lo, ob_hi, ob_lo = (
            sb(n, [P, H, T], F32R, ws) for n in ("oa_hi", "oa_lo", "ob_hi", "ob_lo"))
        x_back = sb("x_back", [P, NT, D], F32, ws)
        sg = [sb(f"sg{n}", [P, T], F32, ws) for n in range(2)]
        ws.close()
        ws = ExitStack()
        x1 = sb("x1", [P, KD, T], F32, ws)
        late = ExitStack()
        fa_hi = sb("fa_hi", [P, 16, T], F32R, late)
        fa_lo = sb("fa_lo", [P, 16, T], F32R, late)
        sqn = [sb(f"sqn{n}", [P, T], F32, late) for n in range(2)]
        rs = sb("rs", [P, T], F32, late)
        late.close()
        late = ExitStack()
        y_tok = sb("y_tok", [P, NT, D], F32, late)
        yg = sb("yg", [P, T], F32, late)
        yT = [sb(f"yT{n}", [P, T], F32, late) for n in range(2)]
        late.close()
        ws.close()

        bank = [ctx.enter_context(nc.psum_tensor(f"bank{b}", [P, T], F32)) for b in range(8)]

        def tiles(b):
            return bank[b][:, :].rearrange("p (t c) -> p t c", c=P)

        dram_line = nc.dram_tensor("bias_line", (H, LINE), F32, kind="Internal").ap()

        w_in0, w_up0, w_down0, gate0, proj0 = w_in[0], w_up[0], w_down[0], w_ple_gate[0], w_ple_proj[0]
        bra0, brb0, wout0 = w_br_a[0], w_br_b[0], w_out[0]
        ss0, rs0, lam_s, nlam, gq8, gsub, alexp = (sm[:, 0:4], sm[:, 4:8], sm[:, 8:10], sm[:, 10:11],
                                                   sm[:, 11:12], sm[:, 12:13], sm[:, 16:24])
        lnx = sm[:, 24:28]
        (G_B, G_A, G_BETA, G_G, G_CUM, G_SUM, G_NEG, G_EXP, G_BEG, G_KD, G_T, G_U) = range(12)

        def gt(n):
            return gates[:, n, :, :]

        def gcols(n, h):
            return gates[:, n, :, bass.ds(h, 1)]

        def dyn(t, i):
            return t[:, bass.ds(i, 1), :].rearrange("p a t -> p (a t)")

        def col(n, i=None):
            return pt[:, n:n + 1] if i is None else pt[:, bass.ds(i + n, 1)]

        arrived = [sem(f"w_arrived{s}") for s in range(4)]
        high_ready, low_ready, product_ready = sem("w_high"), sem("w_low"), sem("product")
        bank_free = [sem(f"bank_read{b}") for b in range(4)]

        block = ctx.enter_context(nc.Block())

        IN_BANKS = (3, 4, 5, 1, 2)

        @block.sync
        def _(sp):
            def load(c, w, col0, k=KD, row0=0):
                if not isinstance(c.number, int):
                    split = sp.to_reg(c.number - 2)
                    sp.wait_ge(sem("consts_in"), 16)
                    sp.wait_ge(low_ready, split)
                elif c.number > 2:
                    sp.wait_ge(low_ready, c.number - 2)
                src = w[row0:row0 + k * P, bass.ds(col0, P)].rearrange("(k p) n -> p k n", p=P)
                sp.dma_start(raw[c.slot][:, 0:k, :], src).then_inc(arrived[c.slot], 16)

            for t in range(NT):
                sp.dma_start(x_tok[:, t, :], x[0, t * P:(t + 1) * P, :]).then_inc(sem(f"x_in{t}"), 16)
                if t == 0:
                    sp.dma_start(sq[:, :], consts[:, 0:C_HOT * P]).then_inc(sem("consts_in"), 16)
            rows = [
                (0, PA_ATTN, attn_norm[0].rearrange("(r c) -> r c", c=P)),
                (0, PA_FFN, ffn_norm[0].rearrange("(r c) -> r c", c=P)),
                (0, PA_PLE, ple_norm[0].rearrange("(r c) -> r c", c=P)),
                (0, PA_CONV, conv_b[0].rearrange("j (r c) -> (j r) c", c=P)),
                (0, PA_SUB, subln_a),
                (0, PA_ON, onorm_b),
                (1, 0, conv_ff[0, 0:2].rearrange("j (r c) -> (j r) c", c=P)),
                (2, 0, conv_ff[0, 2:3].rearrange("j (r c) -> (j r) c", c=P)),
                (2, 2 * KF, conv_ff_bias[0].rearrange("(r c) -> r c", c=P)),
            ]
            for plane, row, src in rows:
                sp.dma_start(prow[row:row + src.shape[0], plane, :], src).then_inc(sem("params_in"), 16)
            for half_ in range(2):
                for row, src in ((PA_QN, qnorm_a), (PA_KN, knorm_a)):
                    sp.dma_start(prow[row:row + 1, 0, half_ * 64:half_ * 64 + 64], src).then_inc(sem("params_in"), 16)
            sp.dma_start(hot[:, :], consts[0:33, C_HOT * P:]).then_inc(sem("small_in"), 16)
            sp.dma_start(tab[0:32, :], rel_bias).then_inc(sem("small_in"), 16)
            sp.dma_start(lamr[:, :, :], lam_a[0].partition_broadcast(P)).then_inc(sem("small_in"), 16)
            sp.dma_start(alog[:, :], a_log_b[0].partition_broadcast(P)).then_inc(sem("small_in"), 16)
            sp.dma_start(dtb[:, :], dt_bias_b[0].partition_broadcast(P)).then_inc(sem("small_in"), 16)

            load(stream.ba.at(0), w_in0, COLS["ba"])
            for n, name in enumerate(("qa", "ka", "va")):
                load(stream.first.at(n), w_in0, COLS[name])
            for n, name in enumerate(LEAD[:3]):
                load(stream.lead.at(n), w_in0, COLS[name] + (AHEAD[name] - 1) * P)
            sp.wait_ge(sem("line_ready"), 1)
            sp.dma_start(dram_line, line[:, :]).then_inc(sem("line_out"), 16)
            sp.wait_ge(sem("line_out"), 16)
            skew = bass.AP(tensor=dram_line.tensor, offset=0, ap=[[1, P], [LINE, H], [1, 256]])
            sp.dma_start(slope[:, :, :], skew).then_inc(sem("slope_in"), 16)
            for n, name in enumerate(LEAD[3:]):
                load(stream.lead.at(3 + n), w_in0, COLS[name] + (AHEAD[name] - 1) * P)
            with sp.Fori(0, H - 2) as h:
                for n, name in enumerate(TURN):
                    load(stream.heads.at(n, h), w_in0, h * P + (COLS[name] + AHEAD[name] * P))
            for n, name in enumerate(LATE):
                load(stream.late.at(n), w_in0, COLS[name] + (H - 2 + AHEAD[name]) * P)
            load(stream.last.at(0), w_in0, COLS["zb"] + (H - 1) * P)
            for seg, gate, branch in ((stream.mix_a, COLS["g0"], bra0), (stream.mix_b, COLS["g1"], brb0)):
                with sp.Fori(0, KD // 2) as n:
                    for q in range(2):
                        load(seg.at(q, n), w_in0, n * (2 * P) + (gate + q * P))
                    for q in range(2):
                        load(seg.at(2 + q, n), branch, n * (2 * P) + q * P)
            sp.wait_ge(sem("ob_done"), H + 1)
            for t in range(NT):
                sp.dma_start(x_back[:, t, :], x[0, t * P:(t + 1) * P, :]).then_inc(sem("x_back_in"), 16)
            with sp.Fori(0, KD // 4) as n:
                for q in range(4):
                    load(stream.out.at(q, n), wout0, n * (4 * P) + q * P)
            for name, part in FFN_ORDER:
                if name == "up":
                    with sp.Fori(0, FFN_PARTS[part] // 2) as n:
                        for q in range(4):
                            first = (FFN_FIRST[part] + q // 2) * P + (q % 2) * FF
                            load(stream.up[part].at(q, n), w_up0, n * (2 * P) + first)
                    if part == 0:
                        sp.wait_ge(product_ready, stream.up[0].first)
                        sp.dma_start(p_tok[:, :, :], p[0, 0].rearrange("(t q) c -> q t c", q=P)).then_inc(sem("p_in"), 16)
                else:
                    with sp.Fori(0, KD // 4) as n:
                        for q in range(4):
                            load(stream.down[part].at(q, n), w_down0, n * (4 * P) + q * P,
                                 FFN_PARTS[part], FFN_FIRST[part] * P)
            with sp.Fori(0, KD // 2) as n:
                for q in range(4):
                    c = stream.ple.at(q, n)
                    if q % 2 == 0:
                        load(c, gate0, n * (2 * P) + (q // 2) * P)
                    else:
                        load(c, proj0, n * (2 * P) + (q // 2) * P, KP)
            with sp.Fori(0, KD) as n:
                sp.wait_ge(sem("y_ready"), n + 1)
                sp.dma_start(out[0, :, bass.ds(n * P, P)].rearrange("(t p) c -> p t c", p=P),
                             y_tok[:, :, bass.ds(n * P, P)]).then_inc(sem("stored"), 16)
            sp.wait_ge(sem("stored"), 16 * KD)

        @block.gpsimd
        def _(pool):
            def split(c, k=KD):
                pool.wait_ge(high_ready, c.number + 1)
                pool.tensor_tensor(wlo[c.slot][:, 0:k, :], raw[c.slot][:, 0:k, :],
                                   whi[c.slot][:, 0:k, :].bitcast(F32), ALU.subtract).then_inc(low_ready, 1)

            def both(c):
                if isinstance(c.number, int):
                    come, multiplied = c.arrival * 16, c.number - 2
                else:
                    come, multiplied = pool.to_reg(c.arrival * 16), pool.to_reg(c.number - 2)
                    pool.wait_ge(sem("consts_in"), 16)
                pool.wait_ge(arrived[c.slot], come)
                pool.wait_ge(product_ready, multiplied)
                pool.tensor_copy(whi[c.slot][:, :, :], raw[c.slot][:, :, :]).then_inc(high_ready, 1)
                split(c)

            for c in [stream.ba.at(0)] + [stream.first.at(n) for n in range(3)] + [stream.lead.at(n) for n in range(3)]:
                split(c)
            for n in range(3, 6):
                both(stream.lead.at(n))
            with pool.Fori(0, H - 2) as h:
                for n in range(7):
                    both(stream.heads.at(n, h))
            for n in range(4):
                both(stream.late.at(n))
            both(stream.last.at(0))
            for n in range(8 + 3):
                both(stream.mix_a.at(n))
            split(stream.mix_a.at(8 + 3))
            for n in range(12, 16):
                split(stream.mix_a.at(n))
            segments = [(stream.mix_b, [KD] * 4), (stream.out, [KD] * 4)]
            for name, part in FFN_ORDER:
                if name == "up":
                    segments.append((stream.up[part], [KD] * 4))
                else:
                    segments.append((stream.down[part], [FFN_PARTS[part]] * 4))
            segments.append((stream.ple, [KD, KP] * 2))
            for seg, ks in segments:
                with pool.Fori(0, seg.turns) as n:
                    for q in range(4):
                        split(seg.at(q, n), ks[q])

        @block.tensor
        def _(pe):
            for name in ("a_turned", "a_scores"):
                pe.sem_inc(sem(name), 1)

            def gemm(c, x_hi, x_lo, k=KD, x0=0, more=None, ready=None):
                pe.wait_ge(low_ready, c.number + 1)
                if not isinstance(c.uses, int) or c.uses > 0:
                    pe.wait_ge(bank_free[c.bank], c.uses)
                acc = bank[c.bank][:, :]
                for i in range(k):
                    if ready is not None:
                        pe.wait_ge(sem(ready[0]), ready[1] + i + 1)
                    for n, (w, xx) in enumerate(((whi, x_hi), (whi, x_lo), (wlo, x_hi))):
                        last = i == k - 1 and n == 2
                        mm = pe.matmul(acc, w[c.slot][:, i, :], xx[:, x0 + i, :],
                                       start=(i == 0 and n == 0), stop=last)
                    if i < k - 1:
                        yield
                if more is not None:
                    mm = more(acc)
                mm.then_inc(product_ready, 1)
                yield

            def run(*gens):
                for g in gens:
                    for _ in g:
                        pass

            class Fill:

                def __init__(self, *gens):
                    self.gens = list(gens)

                def step(self, n=1):
                    for _ in range(n):
                        while self.gens:
                            try:
                                next(self.gens[0])
                                break
                            except StopIteration:
                                self.gens.pop(0)

                def rest(self):
                    while self.gens:
                        self.step()

            pe.wait_ge(sem("consts_in"), 16)
            pe.wait_ge(sem("params_in"), 16 * 13)
            pe.wait_ge(sem("small_in"), 16 * 5)
            pe.wait_ge(sem("tab_set"), 1)
            pe.transpose(bank[7][:, 0:124], prow[0:124, 0, :], ident[0:124, 0:124])
            pe.transpose(bank[7][:, P:P + 88], prow[0:88, 1, :], ident[0:88, 0:88])
            pe.transpose(bank[7][:, 2 * P:2 * P + 88], prow[0:88, 2, :], ident[0:88, 0:88]).then_inc(sem("params_T"), 1)
            pe.matmul(bank[6][0:H, 0:LINE], tab[:, :], hot[:, :], start=True, stop=True).then_inc(sem("line_mm"), 1)
            for c in range(KD):
                if c == 0:
                    for t in range(NT):
                        pe.wait_ge(sem("x_normed"), t + 1)
                if c >= len(IN_BANKS):
                    pe.wait_ge(sem("h_split"), c - len(IN_BANKS) + 1)
                for t in range(NT):
                    mm = pe.transpose(bank[IN_BANKS[c % len(IN_BANKS)]][:, t * P:(t + 1) * P], x_tok[:, t, c * P:(c + 1) * P], ident)
                mm.then_inc(sem("x_T"), 1)

            run(gemm(stream.ba.at(0), hn_hi, hn_lo, ready=("h_split", 0)))
            run(gemm(stream.first.at(0), hn_hi, hn_lo), gemm(stream.first.at(1), hn_hi, hn_lo))
            pe.wait_ge(sem("ba_copied"), 1)
            for t in range(NT):
                mm = pe.transpose(bank[5][:, t * 16:t * 16 + 16], ba_sb[:, t * P:(t + 1) * P], ident[0:16, 0:16])
            mm.then_inc(sem("ba_T"), 1)
            pe.wait_ge(sem("slope_in"), 16)
            pe.wait_ge(sem("line_ready"), 1)
            for n in range(H // 2):
                if n >= 2:
                    pe.wait_ge(sem("bias_ready"), n - 1)
                pe.matmul(bank[6 + n % 2][:, :], flip, slope[:, 2 * n:2 * n + 2, :].rearrange("p a b -> p (a b)"),
                          start=True, stop=True).then_inc(sem("bias_mm"), 1)
            run(gemm(stream.first.at(2), hn_hi, hn_lo))
            pe.wait_ge(sem("g_ready"), 1)
            gg = gates[:, G_G, :, :].rearrange("p t h -> p (t h)")
            pe.matmul(bank[5][:, 64:96], cum, gg, start=True, stop=True)
            pe.matmul(bank[5][:, 96:128], half, gg, start=True, stop=True).then_inc(sem("g_sums"), 1)

            def qk_sum(h, n, c):
                pe.wait_ge(sem("a_sq"), h * 2 + (n + 1))
                pe.matmul(bank[c.bank][:, :], half, sqr[n][:, :], start=True, stop=True).then_inc(sem("a_sum"), 1)

            def v_turn(h):
                pe.wait_ge(sem("va_raw"), h + 1)
                pe.wait_ge(sem("oa_done"), h + 1)
                for t in range(NT):
                    mm = pe.transpose(bank[4][:, t * P:(t + 1) * P], va_raw[:, t * P:(t + 1) * P], ident)
                mm.then_inc(sem("va_T"), 1)

            qk_sum(0, 0, stream.first.at(0))
            qk_sum(0, 1, stream.first.at(1))
            pe.wait_ge(sem("bias_ready"), H // 2)

            def scores(h, i):
                if i == 0:
                    pe.wait_ge(sem("qka_ready"), h * 2 + 3)
                    if not isinstance(h, int) or h > 0:
                        pe.wait_ge(sem("b_r"), h * 2)
                else:
                    pe.wait_ge(sem("a_wT"), h * 4 + i)
                for j in range(2):
                    s = slice(64 * j, 64 * j + 64)
                    mm = pe.matmul(bank[3 + j][:, 0:(i + 1) * P], qa[s, i * P:(i + 1) * P],
                                   ka[s, 0:(i + 1) * P], start=True, stop=True)
                mm.then_inc(sem("a_scores"), 1)

            def turn_w(h, i):
                pe.wait_ge(sem("a_w"), h * 4 + (i + 1))
                for t in range(i + 1):
                    mm = pe.transpose(bank[3][:, t * P:(t + 1) * P], pr[0][:, t * P:(t + 1) * P], ident)
                mm.then_inc(sem("a_turned"), 1)

            def attend(h):
                pe.wait_ge(sem("a_wT"), h * 4 + 4)
                pe.wait_ge(sem("va_ready"), h + 1)
                for t in range(NT):
                    mm = pe.matmul(bank[3][:, t * P:T], va[:, t * P:(t + 1) * P], wT[:, t, t * P:T],
                                   start=(t == 0), stop=(t == NT - 1), skip_group_check=True)
                mm.then_inc(sem("a_out"), 1)

            def b_sum(h, n):
                pe.wait_ge(sem("b_sq"), h * 2 + (n + 1))
                pe.wait_ge(sem("oa_done"), h + 2)
                pe.matmul(bank[3 + n][:, :], ones, sqb[n][:, :], start=True, stop=True).then_inc(sem("b_sum"), 1)

            def turn(h, at, fill, delta=True, attention=True, more_a=True, steps=(3, 6, 5, 2, 2, 3)):
                a = h + 1
                f = Fill(*fill)
                if attention:
                    scores(a, 0)
                f.step(steps[0])
                if delta:
                    pe.wait_ge(sem("qkb_ready"), h * 2 + 2)
                    pe.wait_ge(sem("g_rows_read"), h + 1)
                    for t in range(NT):
                        s = slice(t * P, (t + 1) * P)
                        mm = pe.matmul(tiles(7)[:, t, :], kb[:, s], kb[:, s], start=True, stop=True)
                    mm.then_inc(sem("kk"), 1)
                    for t in range(NT):
                        s = slice(t * P, (t + 1) * P)
                        mm = pe.matmul(tiles(6)[:, t, :], kb[:, s], qb[:, s], start=True, stop=True)
                    mm.then_inc(sem("qk"), 1)
                    pe.wait_ge(sem("ob_done"), h + 1)
                    for t in range(NT):
                        mm = pe.transpose(tiles(5)[:, t, :], bcol[:, t, :], ident)
                    mm.then_inc(sem("b_rows"), 1)
                f.step(steps[1])
                if attention:
                    turn_w(a, 0)
                f.step(1)
                if delta:
                    pe.wait_ge(sem("ct"), h * 6 + 1)
                    for t in range(NT):
                        mm = pe.transpose(tiles(7)[:, t, :], ct[0][:, t, :], ident)
                    mm.then_inc(sem("c1"), 1)
                if attention:
                    scores(a, 1)
                if more_a:
                    qk_sum(h + 2, 0, at("qa"))
                f.step(steps[2])
                if delta:
                    pe.wait_ge(sem("qk_read"), h + 1)
                    for t in range(NT):
                        mm = pe.transpose(tiles(6)[:, t, :], kb[:, t * P:(t + 1) * P], ident)
                    mm.then_inc(sem("kb_T"), 1)
                for n in range(1, 6):
                    if delta:
                        pe.wait_ge(sem("ct"), h * 6 + (n + 1))
                        pe.wait_ge(sem("xi"), h * 5 + n)
                        for t in range(NT):
                            mm = pe.matmul(tiles(7)[:, t, :], ct[n % 2][:, t, :], xi[:, t, :], start=True, stop=True)
                        mm.then_inc(sem("level_u"), 1)
                    f.step(steps[3])
                    if delta:
                        if n == 1:
                            pe.wait_ge(sem("vb_ready"), h + 1)
                            for t in range(NT):
                                mm = pe.transpose(tiles(5)[:, t, :], vb[:, t * P:(t + 1) * P], ident)
                            mm.then_inc(sem("vb_T"), 1)
                            pe.wait_ge(sem("turned_read"), h + 1)
                        pe.wait_ge(sem("ui"), h * 5 + n)
                        pe.wait_ge(sem("xt"), h * 6 + n)
                        if n < 5:
                            for t in range(NT):
                                mm = pe.matmul(tiles(5)[:, t, :], xt[:, t, :], ui[:, t, :], start=True, stop=True)
                            mm.then_inc(sem("level_v"), 1)
                        for t in range(NT):
                            mm = pe.matmul(tiles(6)[:, t, :], ui[:, t, :], xt[:, t, :], start=True, stop=True)
                        mm.then_inc(sem("level_vt"), 1)
                    f.step(steps[4])
                    if n in (2, 4) and attention:
                        turn_w(a, n // 2)
                        f.step(1)
                        scores(a, n // 2 + 1)
                    if n == 2 and more_a:
                        qk_sum(h + 2, 1, at("ka"))
                if delta:
                    pe.wait_ge(sem("xt"), h * 6 + 6)
                    for t in range(NT):
                        mm = pe.matmul(tiles(5)[:, t, :], kbe[:, t, :], xt[:, t, :], start=True, stop=True)
                    mm.then_inc(sem("w_mm"), 1)
                    for t in range(NT):
                        mm = pe.matmul(tiles(7)[:, t, :], xt[:, t, :], vbt[:, t, :], start=True, stop=True)
                    mm.then_inc(sem("u_mm"), 1)
                f.step(steps[5])
                if attention:
                    turn_w(a, 3)
                    v_turn(a)
                for c in range(NC):
                    t, r = c // 2, slice(64 * (c % 2), 64 * (c % 2) + 64)
                    cs = slice(c * CH, (c + 1) * CH)
                    if delta:
                        if c == 0:
                            pe.wait_ge(sem("w_copied"), h + 1)
                        pe.wait_ge(sem("state"), h * 9 + (c + 1))
                        pe.matmul(bank[5][r, 0:P], wt_[:, t, r], state[:, :], start=True, stop=True).then_inc(sem("ws"), 1)
                        pe.matmul(bank[6][:, cs], state[:, :], qeg[:, t, r], start=True, stop=False, skip_group_check=True)
                    f.step(1)
                    if delta:
                        pe.wait_ge(sem("vnew"), h * 8 + (c + 1))
                        pe.matmul(bank[7][:, 0:P], kdec[r, t, :], vnew[r, :], start=True, stop=True).then_inc(sem("kv"), 1)
                        mm = pe.matmul(bank[6][:, cs], vnew[r, :], at_[r, t, r], start=False, stop=True, skip_group_check=True)
                        if c == NC - 1:
                            mm.then_inc(sem("ob_mm"), 1)
                    f.step(1)
                    if c == 0 and attention:
                        attend(a)
                    if c == 2 and attention:
                        pe.wait_ge(sem("oa_sq"), a + 1)
                        pe.matmul(bank[4][:, :], ones, pr[1][:, :], start=True, stop=True).then_inc(sem("oa_sum"), 1)
                    if c == 6 and attention:
                        b_sum(a, 0)
                f.rest()
                if attention:
                    pe.wait_ge(sem("g_cols"), a * 2 + 2)
                    if delta:
                        pe.wait_ge(sem("state"), h * 9 + 9)
                    for t in range(NT):
                        mm = pe.transpose(tiles(7)[:, t, :], gcol[:, t, :], ident)
                    mm.then_inc(sem("g_rows"), 1)
                    b_sum(a, 1)
                if delta:
                    pe.wait_ge(sem("ob_sq"), h + 1)
                    pe.matmul(bank[5][:, :], ones, sqo[:, :], start=True, stop=True).then_inc(sem("ob_sum"), 1)

            def fill_of(seg, names, h=0):
                return [gemm(seg.at(n, h), hn_hi, hn_lo) for n in range(len(names))]

            def place(seg, names, h=0):
                return lambda name: seg.at(names.index(name), h)

            turn(-1, place(stream.lead, LEAD), fill_of(stream.lead, LEAD), delta=False)
            with pe.Fori(0, H - 2) as h:
                turn(h, place(stream.heads, TURN, h), fill_of(stream.heads, TURN, h))
            turn(H - 2, place(stream.late, LATE), fill_of(stream.late, LATE), more_a=False)
            pe.wait_ge(sem("b_r"), H * 2)
            fill = [gemm(stream.last.at(0), hn_hi, hn_lo)]
            for n in range(2):
                fill += [gemm(stream.mix_a.at(q, n), hn_hi, hn_lo) for q in range(2)]
                fill += [gemm(stream.mix_a.at(2 + q, n), oa_hi, oa_lo, ready=("o_split", 0) if n + q == 0 else None)
                         for q in range(2)]
            turn(H - 1, None, fill, attention=False, more_a=False, steps=(4, 8, 6, 3, 3, 4))

            def mix(seg, n, hi, lo, ready=None):
                for q in range(2):
                    run(gemm(seg.at(q, n), hn_hi, hn_lo))
                for q in range(2):
                    run(gemm(seg.at(2 + q, n), hi, lo, ready=ready if q == 0 else None))

            with pe.Fori(2, KD // 2) as n:
                mix(stream.mix_a, n, oa_hi, oa_lo)
            mix(stream.mix_b, 0, ob_hi, ob_lo, ready=("o_split", H))
            with pe.Fori(1, KD // 2) as n:
                mix(stream.mix_b, n, ob_hi, ob_lo)
            pe.wait_ge(sem("x_back_in"), 16 * NT)

            def norm_sum(stage, c):
                pe.wait_ge(sem("n_sq"), stage * KD + c + 1)
                pe.matmul(bank[4][:, :], ones, (sqn, (s0, tn))[stage][c % 2][:, :], start=(c == 0),
                          stop=(c == KD - 1)).then_inc(sem("n_sum"), 1)

            for n in range(KD):
                c = stream.out.at(n % 4, n // 4)

                def residual(acc, n=n):
                    for t in range(NT):
                        mm = pe.matmul(acc[:, t * P:(t + 1) * P], x_back[:, t, n * P:(n + 1) * P], ident,
                                       start=False, stop=True, skip_group_check=True)
                    return mm
                run(gemm(c, mx_hi, mx_lo, more=residual, ready=("gb_used", 2) if n == 0 else None))
                if n > 0:
                    norm_sum(0, n - 1)
            norm_sum(0, KD - 1)
            pe.wait_ge(sem("n_split"), KD)
            for name, part in FFN_ORDER:
                first_k, k = 8 * FFN_HALF[part], FFN_PARTS[part]
                if name == "up":
                    with pe.Fori(0, k // 2) as n:
                        for q in range(4):
                            run(gemm(stream.up[part].at(q, n), hn_hi, hn_lo))
                    if part == 0:
                        pe.wait_ge(sem("p_in"), 16)
                        for c in range(KP):
                            for t in range(NT):
                                mm = pe.transpose(tiles(5 + c)[:, t, :], p_tok[:, t, c * P:(c + 1) * P], ident)
                            mm.then_inc(sem("p_T"), 1)
                else:
                    pe.wait_ge(sem("fa_lo"), FFN_FIRST[part] + k)
                    if part < 2:
                        with pe.Fori(0, KD // 4) as n:
                            for q in range(4):
                                run(gemm(stream.down[part].at(q, n), fa_hi, fa_lo, k, first_k))
                    else:
                        for n in range(KD):
                            run(gemm(stream.down[part].at(n), fa_hi, fa_lo, k, first_k))
                            if n > 0:
                                norm_sum(1, n - 1)
            norm_sum(1, KD - 1)
            pe.wait_ge(sem("n_split"), 2 * KD)
            pe.wait_ge(sem("p_split"), KP)

            def turn_y(c, q):
                pe.wait_ge(sem("yT"), c + 2)
                for t in range(NT):
                    mm = pe.transpose(tiles(5)[:, t, :], yT[q][:, t * P:(t + 1) * P], ident)
                mm.then_inc(sem("y_T"), 1)

            def ple(n, q):
                run(gemm(stream.ple.at(2 * q, n), hn_hi, hn_lo))
                run(gemm(stream.ple.at(2 * q + 1, n), p_hi, p_lo, KP))

            ple(0, 0)
            with pe.Fori(0, KD // 2 - 1) as n:
                for q in range(2):
                    ple(n, 1 + q)
                    turn_y(2 * n + q, q)
            ple(KD // 2 - 1, 1)
            turn_y(KD - 2, 0)
            turn_y(KD - 1, 1)

        @block.scalar
        def _(act):
            act.sem_inc(sem("a_exp"), 1)

            def done(ins, name, value):
                ins.then_inc(sem(name) if isinstance(name, str) else name, 1)
                act.wait_ge(sem(name) if isinstance(name, str) else name, value)

            def rsqrt(dst, src, scale, names, value):
                done(nc.scalar.activation(dst, src, ACT.Ln, bias=sm[:, 28:29], scale=scale), names[0], value)
                done(nc.scalar.activation(dst, dst, ACT.Exp, scale=-0.5), names[1], value)

            def high(c):
                act.wait_ge(arrived[c.slot], c.arrival * 16)
                if not isinstance(c.number, int) or c.number > 2:
                    act.wait_ge(product_ready, c.number - 2)
                done(nc.scalar.activation(whi[c.slot][:, :, :], raw[c.slot][:, :, :], ACT.Copy), high_ready, c.number + 1)

            act.preload_act_table_set("natural_log_exp_and_others")
            act.wait_ge(sem("eps_set"), 1)
            for t in range(NT):
                act.wait_ge(sem(f"x_in{t}"), 16)
                done(nc.scalar.activation(junk[:, :], x_tok[:, t, :], ACT.Square, accum_out=ss0[:, t:t + 1]),
                     "x_sq", t + 1)
            done(nc.scalar.activation(lnx, ss0, ACT.Ln, bias=sm[:, 28:29], scale=1.0 / D), "x_ln", 1)
            done(nc.scalar.activation(rs0, lnx, ACT.Exp, scale=-0.5), "x_r", 1)
            act.wait_ge(sem("lam_sum"), 1)
            done(nc.scalar.activation(lam_s, lam_s, ACT.Exp), "lam_exp", 1)
            done(nc.scalar.activation(alexp, alog[:, :], ACT.Exp), "a_exp0", 1)
            act.wait_ge(sem("pt_ready"), 1)
            for c in range(KD):
                act.wait_ge(sem("x_T"), c + 1)
                done(nc.scalar.activation(hn_hi[:, c, :], bank[IN_BANKS[c % len(IN_BANKS)]][:, :], ACT.Copy,
                                          scale=pt[:, PA_ATTN + c:PA_ATTN + c + 1]), "h_high", c + 1)
                if c == 4:
                    high(stream.ba.at(0))

            def prep_qk(h, n, c):
                dst = (qa_raw, ka_raw)[n]
                act.wait_ge(product_ready, c.number + 1)
                act.wait_ge(sem("qka_ready"), h * 2 + 1)
                done(nc.scalar.activation(dst[:, :], bank[c.bank][:, :], ACT.Copy), "qka_raw", h * 2 + (n + 1))
                done(nc.scalar.activation(sqr[n][:, :], dst[:, :], ACT.Square), "a_sq", h * 2 + (n + 1))

            def prep_r(h, n, c):
                act.wait_ge(sem("a_sum"), h * 2 + (n + 1))
                done(nc.scalar.activation(sqr[n][:, :], bank[c.bank][:, :], ACT.Ln, bias=sm[:, 28:29], scale=1.0 / 64),
                     bank_free[c.bank], c.uses + 1)
                done(nc.scalar.activation(sqr[n][:, :], sqr[n][:, :], ACT.Exp, scale=-0.5), "a_r", h * 2 + (n + 1))

            def prep_v(h, c):
                act.wait_ge(product_ready, c.number + 1)
                done(nc.scalar.activation(va_raw[:, :], bank[c.bank][:, :], ACT.Copy), bank_free[c.bank], c.uses + 1)
                act.sem_inc(sem("va_raw"), 1)

            def v_copy(h):
                act.wait_ge(sem("va_T"), h + 1)
                done(nc.scalar.activation(va[:, :], bank[4][:, :], ACT.Copy), "va_ready", h + 1)

            for c in (stream.first.at(0), stream.first.at(1), stream.first.at(2)):
                high(c)
            prep_qk(0, 0, stream.first.at(0))
            high(stream.lead.at(0))
            def plane(n):
                return gates[:, n, :, :].rearrange("p t h -> p (t h)")
            act.wait_ge(sem("ba_planes"), 2)
            done(nc.scalar.activation(plane(G_BETA), plane(G_B), ACT.Exp, scale=-1.0), "beta_exp", 1)
            done(nc.scalar.activation(plane(G_T), plane(G_A), ACT.Abs), "soft", 1)
            done(nc.scalar.activation(plane(G_U), plane(G_T), ACT.Exp, scale=-1.0), "soft", 2)
            done(nc.scalar.activation(plane(G_T), plane(G_U), ACT.Ln, bias=sm[:, 29:30]), "soft", 3)
            prep_qk(0, 1, stream.first.at(1))
            high(stream.lead.at(1))
            prep_v(0, stream.first.at(2))
            high(stream.lead.at(2))
            act.wait_ge(sem("g_cum"), 1)
            done(nc.scalar.activation(plane(G_EXP), plane(G_CUM), ACT.Exp), "g_exp", 1)
            act.wait_ge(sem("g_rest"), 1)
            done(nc.scalar.activation(plane(G_KD), plane(G_T), ACT.Exp), "g_kd", 1)
            prep_r(0, 0, stream.first.at(0))
            prep_r(0, 1, stream.first.at(1))

            def softmax(h, i):
                w = (i + 1) * P
                act.wait_ge(sem("a_nmax"), h * 4 + (i + 1))
                act.wait_ge(sem("a_turned"), h * 4 + i + 1)
                for j in range(2):
                    done(nc.scalar.activation(pr[j][:, 0:w], bank[3 + j][:, 0:w], ACT.Exp,
                                              bias=ast[:, 2 + j:3 + j], accum_out=ast[:, 4 + j:5 + j]),
                         "a_exp", h * 8 + (2 * i + j + 1) + 1)

            def keep_w(h, i):
                act.wait_ge(sem("a_turned"), h * 4 + (i + 1) + 1)
                done(nc.scalar.activation(wT[:, 0:i + 1, i * P:(i + 1) * P], tiles(3)[:, 0:i + 1, :], ACT.Copy),
                     "a_wT", h * 4 + (i + 1))

            def finish_sigmoid(h, n):
                done(nc.scalar.activation(silu[:, :], silu[:, :], ACT.Ln, bias=sm[:, 29:30]), "b_log", h * 4 + (n + 1))
                done(nc.scalar.activation(silu[:, :], silu[:, :], ACT.Exp, scale=-1.0), "b_sigmoid", h * 4 + (n + 1))

            def silu_exp(h, n):
                act.wait_ge(sem("b_conv"), h * 3 + (n + 1))
                done(nc.scalar.activation(silu[:, :], (qb, kb, vb)[n][:, :], ACT.Exp, scale=-1.0),
                     "b_exp", h * 3 + (n + 1))
                finish_sigmoid(h, n)

            def square_b(h, n):
                act.wait_ge(sem("b_silu"), h * 2 + (n + 1))
                done(nc.scalar.activation(sqb[n][:, :], (qb, kb)[n][:, :], ACT.Square), "b_sq", h * 2 + (n + 1))

            def turn(h, at, delta=True, attention=True, more_a=True):
                a = h + 1
                if delta:
                    act.wait_ge(sem("dec_arg"), h + 1)
                    done(nc.scalar.activation(dec[:, :, :], dec[:, :, :], ACT.Exp), "dec", h + 1)
                if not attention:
                    act.wait_ge(sem("oa_done"), H + 1)
                    for k in range(H):
                        done(nc.scalar.activation(oa_hi[:, k, :], o_a[:, k, :], ACT.Copy), "o_high", k + 1)
                if attention:
                    softmax(a, 0)
                if more_a:
                    prep_qk(h + 2, 0, at("qa"))
                if attention:
                    keep_w(a, 0)
                if delta:
                    silu_exp(h, 2)
                if attention:
                    softmax(a, 1)
                if more_a:
                    prep_r(h + 2, 0, at("qa"))
                for n in range(1, 6):
                    if delta:
                        act.wait_ge(sem("level_u"), h * 5 + n)
                        done(nc.scalar.activation(ui[:, :, :], tiles(7), ACT.Copy), "ui", h * 5 + n)
                    if n == 1 and more_a:
                        prep_qk(h + 2, 1, at("ka"))
                    if n == 2 and attention:
                        keep_w(a, 1)
                    if n == (2 if attention else 1):
                        if delta:
                            c = at("zb")
                            act.wait_ge(product_ready, c.number + 1)
                            act.wait_ge(sem("vb_ready"), h + 1)
                            act.wait_ge(sem("ob_done"), h + 1)
                            done(nc.scalar.activation(zb[:, :], bank[c.bank][:, :], ACT.Copy), "zb_raw", h + 1)
                            done(nc.scalar.activation(silu[:, :], bank[c.bank][:, :], ACT.Exp, scale=-1.0),
                                 bank_free[c.bank], c.uses + 1)
                            finish_sigmoid(h, 3)
                    if n == 3:
                        if attention:
                            softmax(a, 2)
                        if more_a:
                            prep_r(h + 2, 1, at("ka"))
                    if n == 4 and attention:
                        keep_w(a, 2)
                    if n == 5 and attention:
                        softmax(a, 3)
                    if n in (1, 3) and not attention:
                        gate_a(n // 2)
                if delta:
                    act.wait_ge(sem("w_mm"), h + 1)
                    done(nc.scalar.activation(wt_[:, :, :], tiles(5), ACT.Copy), "w_copied", h + 1)
                if not attention:
                    gate_a(2)
                    gate_a(3)
                if attention:
                    keep_w(a, 3)
                    v_copy(a)
                    act.wait_ge(sem("a_out"), a + 1)
                    done(nc.scalar.activation(pr[1][:, :], bank[3][:, :], ACT.Square), "oa_sq", a + 1)
                    silu_exp(h + 1, 0)
                    act.wait_ge(sem("oa_sum"), a + 1)
                    rsqrt(pr[1][:, :], bank[4][:, :], 1.0 / P, ("oa_ln", "oa_r"), a + 1)
                    square_b(a, 0)
                    silu_exp(a, 1)
                    square_b(a, 1)
                    b_r(a, 0)
                if delta:
                    act.wait_ge(sem("ob_mm"), h + 1)
                    done(nc.scalar.activation(sqo[:, :], bank[6][:, :], ACT.Square), "ob_sq", h + 1)
                if attention:
                    act.wait_ge(sem("g_rows"), a + 1)
                    done(nc.scalar.activation(eg[:, :, :].rearrange("p t c -> p (t c)"), bank[7][:, :], ACT.Exp), "eg", a + 1)
                    b_r(a, 1)
                if more_a:
                    prep_v(h + 2, at("va"))
                if delta:
                    act.wait_ge(sem("ob_sum"), h + 1)
                    rsqrt(sqo[:, :], bank[5][:, :], 1.0 / P, ("ob_sum_read", "ob_r"), h + 1)

            def gate_a(n):
                c, g = stream.mix_a.at(n % 2, n // 2), sqr[n % 2][:, :]
                act.wait_ge(product_ready, c.number + 1)
                if n >= 2:
                    act.wait_ge(sem("ga_used"), n - 1)
                done(nc.scalar.activation(g, bank[c.bank][:, :], ACT.Exp, scale=-1.0), bank_free[c.bank], c.uses + 1)
                done(nc.scalar.activation(g, g, ACT.Ln, bias=sm[:, 29:30]), "ga_log", n + 1)
                done(nc.scalar.activation(g, g, ACT.Exp, scale=-1.0), "ga_made", n + 1)

            def b_r(h, n):
                act.wait_ge(sem("b_sum"), h * 2 + (n + 1))
                rsqrt(sqb[n][:, :], bank[3 + n][:, :], 1.0, ("b_ln", "b_r"), h * 2 + (n + 1))

            def place(seg, names, h=0):
                return lambda name: seg.at(names.index(name), h)

            turn(-1, place(stream.lead, LEAD), delta=False)
            with act.Fori(0, H - 2) as h:
                turn(h, place(stream.heads, TURN, h))
            turn(H - 2, place(stream.late, LATE), more_a=False)
            turn(H - 1, place(stream.last, LAST), attention=False, more_a=False)

            act.wait_ge(sem("ob_done"), H + 1)
            act.wait_ge(sem("ga_used"), 4)
            for k in range(H):
                done(nc.scalar.activation(ob_hi[:, k, :], o_b[:, k, :], ACT.Copy), "o_high", H + k + 1)
            act.wait_ge(low_ready, stream.mix_a.at(3, 2).number)

            def mix(seg, n, made, used, ahead):
                for q in range(2):
                    c = seg.at(q, n)
                    act.wait_ge(product_ready, c.number + 1)
                    act.wait_ge(sem(used), n * 2 + (q - 1 + ahead))
                    done(nc.scalar.activation(sg[q][:, :], bank[c.bank][:, :], ACT.Sigmoid), bank_free[c.bank], c.uses + 1)
                    act.sem_inc(sem(made), 1)
                    high(seg.at(q + 3, n))
                for q in range(2, 4):
                    high(seg.at(q + 3, n))

            with act.Fori(2, KD // 2) as n:
                mix(stream.mix_a, n, "ga_made", "ga_used", 0)
            act.wait_ge(sem("ga_used"), KD)
            with act.Fori(0, KD // 2) as n:
                mix(stream.mix_b, n, "gb_made", "gb_used", 2)
            for n in range(KD):
                c = stream.out.at(n % 4, n // 4)
                act.wait_ge(product_ready, c.number + 1)
                src = bank[c.bank][:, :]
                done(nc.scalar.activation(x1[:, n, :], src, ACT.Copy), "x1_ready", n + 1)
                done(nc.scalar.activation(hn_hi[:, n, :], src, ACT.Copy, scale=pt[:, PA_FFN + n:PA_FFN + n + 1]),
                     "n_high", n + 1)
                if n >= 2:
                    act.wait_ge(sem("n_sum"), n - 1)
                if n == 0:
                    act.wait_ge(product_ready, stream.out.first)
                done(nc.scalar.activation(sqn[n % 2][:, :], src, ACT.Square), bank_free[c.bank], c.uses + 1)
                act.sem_inc(sem("n_sq"), 1)
                high(stream.out.at(n + 3))

            def norm_r(stage):
                act.wait_ge(sem("n_sum"), (stage + 1) * KD)
                rsqrt(rs[:, :], bank[4][:, :], 1.0 / D, ("n_ln", "n_r"), stage + 1)

            norm_r(0)
            for name, part in FFN_ORDER:
                if name == "up":
                    seg = stream.up[part]
                    with act.Fori(0, seg.turns) as n:
                        for q in range(2):
                            high(seg.at(2 * q + 3, n))
                            act.wait_ge(sem("u_conv"), n * 2 + (FFN_FIRST[part] + q + 1))
                            done(nc.scalar.activation(s0[:, :], u0[:, :], ACT.Sigmoid), "u_sig",
                                 n * 2 + (FFN_FIRST[part] + q + 1))
                            high(seg.at(2 * q + 4, n))
                    if part == 0:
                        for c in range(KP):
                            act.wait_ge(sem("p_T"), c + 1)
                            done(nc.scalar.activation(p_hi[:, c, :], bank[5 + c][:, :], ACT.Copy), "p_high", c + 1)
                else:
                    with act.Fori(0, stream.down[part].turns) as n:
                        for q in range(4):
                            high(stream.down[part].at(q + 3, n))
            norm_r(1)

            def ple_turn(n, ahead):
                for q in range(4):
                    if q < ahead:
                        high(stream.ple.at(q + 3, n))
                    if q % 2 == 0:
                        k = n * 2 + q // 2
                        act.wait_ge(sem("gate_scaled"), k + 1)
                        done(nc.scalar.activation(yg[:, :], yg[:, :], ACT.Sigmoid), "gate", k + 1)

            with act.Fori(0, KD // 2 - 1) as n:
                ple_turn(n, 4)
            ple_turn(KD // 2 - 1, 1)

        @block.vector
        def _(dve):
            for name in ("ob_done", "qka_ready", "oa_done", "yT"):
                dve.sem_inc(sem(name), 1)
            dve.sem_inc(sem("gb_used"), 2)
            dve.sem_inc(bank_free[3], 1)
            links = [0, 0, 0]

            def done(ins, name, value):
                ins.then_inc(sem(name) if isinstance(name, str) else name, 1)
                dve.wait_ge(sem(name) if isinstance(name, str) else name, value)

            def link(ins):
                links[2] += 1
                ins.then_inc(sem("vector_step"), 1)
                dve.wait_ge(sem("vector_step"), links[0] + links[2])

            def section():
                links[0], links[2] = links[0] + links[2], 0

            def loop(turns, body):
                section()
                base = links[0]
                per = LINKS[body]
                with dve.Fori(0, turns) as i:
                    links[0], links[2] = i * per + base, 0
                    body(i)
                assert links[2] == per, (links, per)
                links[0], links[2] = base + per * turns, 0

            V = nc.vector

            done(V.memset(sm[:, 28:29], EPS), "eps_set0", 1)
            done(V.memset(sm[:, 29:30], 1.0), "eps_set", 1)
            done(V.memset(tab[32:33, :], NEG), "tab_set", 1)
            dve.wait_ge(sem("params_in"), 16 * 13)
            dve.wait_ge(sem("small_in"), 16 * 5)
            link(V.tensor_tensor(lamp[:, :, :], lamr[:, 0:4:2, :], lamr[:, 1:4:2, :], ALU.mult))
            done(V.tensor_reduce(lam_s, lamp[:, :, :], AX_X, ALU.add), "lam_sum", 1)
            dve.wait_ge(sem("x_r"), 1)
            for t in range(NT):
                done(V.tensor_scalar(x_tok[:, t, :], x_tok[:, t, :], rs0[:, t:t + 1], None, ALU.mult), "x_normed", t + 1)
            dve.wait_ge(sem("params_T"), 1)
            link(V.tensor_copy(pt[:, 0:124], bank[7][:, 0:124]))
            link(V.tensor_copy(pt[:, P:P + 88], bank[7][:, P:P + 88]))
            done(V.tensor_copy(pt[:, 2 * P:2 * P + 88], bank[7][:, 2 * P:2 * P + 88]), "pt_ready", 1)
            dve.wait_ge(sem("line_mm"), 1)
            done(V.tensor_copy(line[:, :], bank[6][0:H, 0:LINE]), "line_ready", 1)
            for c in range(KD):
                dve.wait_ge(sem("h_high"), c + 1)
                done(V.scalar_tensor_tensor(out=hn_lo[:, c, :], in0=bank[IN_BANKS[c % len(IN_BANKS)]][:, :],
                                            scalar=pt[:, PA_ATTN + c:PA_ATTN + c + 1],
                                            in1=hn_hi[:, c, :].bitcast(F32), op0=ALU.mult, op1=ALU.subtract),
                     "h_split", c + 1)
            dve.wait_ge(sem("lam_exp"), 1)
            link(V.tensor_scalar(nlam, lam_s[:, 1:2], lam_s[:, 0:1], -LAM_INIT, ALU.subtract, ALU.add))
            link(V.tensor_scalar(gq8, pt[:, PA_QN:PA_QN + 1], 64 ** -0.5, None, ALU.mult))
            link(V.tensor_scalar(gsub, pt[:, PA_SUB:PA_SUB + 1], 1.0 - LAM_INIT, None, ALU.mult))
            c = stream.ba.at(0)
            dve.wait_ge(product_ready, c.number + 1)
            link(V.tensor_copy(ba_sb[:, :], bank[c.bank][0:16, :]))
            done(V.tensor_copy(ba_sb[:, 0:1], ba_sb[:, 0:1]), "ba_copied", 1)
            dve.sem_inc(bank_free[c.bank], 1)
            dve.wait_ge(sem("ba_T"), 1)
            turned = bank[5][:, 0:64].rearrange("p (t c) -> p t c", c=16)
            done(V.tensor_copy(gt(G_B), turned[:, :, 0:H]), "ba_planes", 1)
            dve.wait_ge(sem("a_exp0"), 1)
            done(V.tensor_tensor(gt(G_A), turned[:, :, H:2 * H],
                                 dtb[:, :].unsqueeze(1).to_broadcast([P, NT, H]), ALU.add), "ba_planes", 2)
            for n in range(H // 2):
                dve.wait_ge(sem("bias_mm"), n + 1)
                done(V.tensor_copy(bias[:, 2 * n:2 * n + 2, :].rearrange("p a b -> p (a b)"), bank[6 + n % 2][:, :]),
                     "bias_ready", n + 1)
            dve.wait_ge(sem("soft"), 3)
            link(V.tensor_scalar(gt(G_BETA), gt(G_BETA), 1.0, None, ALU.add))
            link(V.reciprocal(gt(G_BETA), gt(G_BETA)))
            link(V.scalar_tensor_tensor(out=gt(G_U), in0=gt(G_A), scalar=0.0, in1=gt(G_T), op0=ALU.max, op1=ALU.add))
            done(V.scalar_tensor_tensor(out=gt(G_G), in0=gt(G_U), scalar=-1.0,
                                        in1=alexp.unsqueeze(1).to_broadcast([P, NT, H]), op0=ALU.mult, op1=ALU.mult),
                 "g_ready", 1)
            dve.wait_ge(sem("g_sums"), 1)
            done(V.tensor_copy(gates[:, G_CUM, :, :].rearrange("p t h -> p (t h)"), bank[5][:, 64:96]), "g_cum", 1)
            done(V.tensor_tensor(gates[:, G_T, :, :].rearrange("p t h -> p (t h)"), bank[5][:, 96:128],
                                 gates[:, G_CUM, :, :].rearrange("p t h -> p (t h)"), ALU.subtract), "g_rest", 1)
            dve.wait_ge(sem("g_kd"), 1)
            link(V.tensor_tensor(gt(G_BEG), gt(G_BETA), gt(G_EXP), ALU.mult))

            def prep(h, n):
                dve.wait_ge(sem("a_r"), h * 2 + (n + 1))
                dve.wait_ge(sem("a_scores"), h * 4 + 1)
                done(V.scalar_tensor_tensor(out=(qa, ka)[n][:, :], in0=(qa_raw, ka_raw)[n][:, :],
                                            scalar=(gq8, pt[:, PA_KN:PA_KN + 1])[n], in1=sqr[n][:, :],
                                            op0=ALU.mult, op1=ALU.mult), "qka_ready", h * 2 + (n + 1) + 1)

            def maxima(h, i):
                w, near = (i + 1) * P, min(i + 1, 2) * P
                dve.wait_ge(sem("a_scores"), h * 4 + (i + 1) + 1)
                for j in range(2):
                    b = bank[3 + j]
                    link(V.tensor_tensor(b[:, w - near:w], b[:, w - near:w], bias_of(h, near), ALU.add))
                dve.wait_ge(sem("a_exp"), h * 8 + 2 * i + 1)
                for j in range(2):
                    link(V.tensor_reduce(ast[:, j:j + 1], bank[3 + j][:, 0:w], AX_X, ALU.max))
                done(V.tensor_scalar(ast[:, 2:4], ast[:, 0:2], -1.0, None, ALU.mult), "a_nmax", h * 4 + (i + 1))

            def bias_of(h, near):
                return bias[:, bass.ds(h, 1), 256 - near:256].rearrange("p a b -> p (a b)")

            def combine(h, i):
                w = (i + 1) * P
                dve.wait_ge(sem("a_exp"), h * 8 + (2 * i + 2) + 1)
                link(V.reciprocal(ast[:, 6:8], ast[:, 4:6]))
                link(V.tensor_scalar(ast[:, 8:9], ast[:, 7:8], nlam, None, ALU.mult))
                link(V.tensor_scalar(pr[1][:, 0:w], pr[1][:, 0:w], ast[:, 8:9], None, ALU.mult))
                done(V.scalar_tensor_tensor(out=pr[0][:, 0:w], in0=pr[0][:, 0:w], scalar=ast[:, 6:7],
                                            in1=pr[1][:, 0:w], op0=ALU.mult, op1=ALU.add), "a_w", h * 4 + (i + 1))

            def conv(h, n, c):
                y, src = (qb, kb, vb)[n], bank[c.bank]

                def tap(j):
                    return col(PA_CONV + 24 * j + 8 * n, h)

                def start():
                    dve.wait_ge(product_ready, c.number + 1)
                    link(V.tensor_scalar(y[:, :], src[:, :], tap(3), None, ALU.mult))

                def middle(j):
                    back = 3 - j
                    link(V.scalar_tensor_tensor(out=y[:, back:], in0=src[:, 0:T - back], scalar=tap(j),
                                                in1=y[:, back:], op0=ALU.mult, op1=ALU.add))

                def end():
                    done(V.scalar_tensor_tensor(out=y[:, 3:], in0=src[:, 0:T - 3], scalar=tap(0),
                                                in1=y[:, 3:], op0=ALU.mult, op1=ALU.add), bank_free[c.bank], c.uses + 1)
                    dve.sem_inc(sem("b_conv"), 1)
                return [start, lambda: middle(2), lambda: middle(1), end]

            def finish_silu(h, n):
                y = (qb, kb, vb)[n]

                def end():
                    dve.wait_ge(sem("b_sigmoid"), h * 4 + (n + 1))
                    done(V.tensor_tensor(y[:, :], y[:, :], silu[:, :], ALU.mult), *(
                        ("b_silu", h * 2 + (n + 1)) if n < 2 else ("vb_ready", h + 1)))
                return [end]

            def steps(*lists):
                for some in lists:
                    for step in some:
                        step()

            def flat(t):
                return t[:, :, :].rearrange("p t c -> p (t c)")

            def level_mask(n):
                return const(C_LEVEL + n).unsqueeze(1).to_broadcast([P, NT, P])

            def make_ct(h, n):
                done(V.tensor_tensor(ct[n % 2][:, :, :], lt[:, :, :], level_mask(n), ALU.mult), "ct", h * 6 + (n + 1))

            def head_start(h):
                for n, scale in ((0, P ** -0.5), (1, 1.0)):
                    dve.wait_ge(sem("b_r"), h * 2 + (n + 1))
                    y = (qb, kb)[n]
                    done(V.scalar_tensor_tensor(out=y[:, :], in0=y[:, :], scalar=scale, in1=sqb[n][:, :],
                                                op0=ALU.mult, op1=ALU.mult), "qkb_ready", h * 2 + (n + 1))
                dve.wait_ge(sem("eg"), h + 1)
                for t in range(NT):
                    ins = V.scalar_tensor_tensor(out=dec[:, t, :], in0=tiles(7)[:, t, :],
                                                 scalar=gates[:, G_CUM, t, bass.ds(h, 1)], in1=mask,
                                                 op0=ALU.subtract, op1=ALU.add)
                    if t < NT - 1:
                        link(ins)
                    else:
                        done(ins, "g_rows_read", h + 1)
                        dve.sem_inc(sem("dec_arg"), 1)

            def turn(h, at, vb_at, delta=True, attention=True, more_a=True):
                a = h + 1
                if attention:
                    maxima(a, 0)
                if delta:
                    dve.wait_ge(sem("dec"), h + 1)
                    dve.wait_ge(sem("b_rows"), h + 1)
                    link(V.tensor_tensor(flat(decb), flat(dec), bank[5][:, :], ALU.mult))
                    dve.wait_ge(sem("kk"), h + 1)
                    link(V.tensor_tensor(flat(lt), bank[7][:, :], flat(decb), ALU.mult))
                    make_ct(h, 0)
                    link(V.tensor_tensor(flat(qeg), qb[:, :], flat(eg), ALU.mult))
                if attention:
                    combine(a, 0)
                if delta:
                    done(V.tensor_tensor(xt[:, :, :], ident.unsqueeze(1).to_broadcast([P, NT, P]), ct[0][:, :, :],
                                         ALU.subtract), "xt", h * 6 + 1)
                    make_ct(h, 1)
                    dve.wait_ge(sem("qk"), h + 1)
                    done(V.tensor_tensor(flat(at_), bank[6][:, :], flat(dec), ALU.mult), "qk_read", h + 1)
                    steps(conv(h, 2, vb_at))
                if not attention:
                    low_a(range(4))
                if delta:
                    dve.wait_ge(sem("c1"), h + 1)
                    done(V.tensor_tensor(xi[:, :, :], ident.unsqueeze(1).to_broadcast([P, NT, P]), tiles(7),
                                         ALU.subtract), "xi", h * 5 + 1)
                if attention:
                    maxima(a, 1)
                if delta:
                    steps(finish_silu(h, 2))
                    dve.wait_ge(sem("kb_T"), h + 1)
                    link(V.tensor_tensor(kbe[:, :, :], tiles(6), gcols(G_BEG, h).to_broadcast([P, NT, P]), ALU.mult))
                    link(V.tensor_tensor(kdec[:, :, :], tiles(6), gcols(G_KD, h).to_broadcast([P, NT, P]), ALU.mult))
                    dve.wait_ge(sem("vb_T"), h + 1)
                    done(V.tensor_tensor(vbt[:, :, :], tiles(5), gcols(G_BETA, h).to_broadcast([P, NT, P]), ALU.mult),
                         "turned_read", h + 1)
                side = []
                if attention:
                    q, k = conv(a, 0, at("qb")), conv(a, 1, at("kb"))
                    side = q + k[0:2] + g_steps(a) + finish_silu(a, 0) + k[2:] + finish_silu(a, 1)
                for n in range(1, 6):
                    if delta:
                        if n < 5:
                            make_ct(h, n + 1)
                            dve.wait_ge(sem("level_v"), h * 4 + n)
                            done(V.tensor_tensor(xi[:, :, :], xi[:, :, :], tiles(5), ALU.subtract), "xi", h * 5 + (n + 1))
                        dve.wait_ge(sem("level_vt"), h * 5 + n)
                        done(V.tensor_tensor(xt[:, :, :], xt[:, :, :], tiles(6), ALU.subtract), "xt", h * 6 + (n + 1))
                    if attention:
                        if n in (1, 3, 5):
                            combine(a, (n + 1) // 2)
                        else:
                            maxima(a, n // 2 + 1)
                    if n == 4 and delta:
                        dve.wait_ge(sem("b_sigmoid"), h * 4 + 4)
                        link(V.tensor_tensor(zb[:, :], zb[:, :], silu[:, :], ALU.mult))
                    if n == 4 and more_a:
                        prep(h + 2, 0)
                    if not attention:
                        if n in (1, 2):
                            low_a(range(2 * n + 2, 2 * n + 4))
                        if n in (4, 5):
                            mix_a(n - 4, stream.mix_a.at(2 + n - 4), sqr[n - 4])
                    if n == 2 and not delta:
                        for _ in range(4):
                            side.pop(0)()
                if delta:
                    done(V.memset(state[:, :], 0.0), "state", h * 9 + 1)
                    dve.wait_ge(sem("u_mm"), h + 1)
                    link(V.tensor_copy(flat(us), bank[7][:, :]))
                for c in range(NC):
                    t, r = c // 2, slice(64 * (c % 2), 64 * (c % 2) + 64)
                    if delta:
                        dve.wait_ge(sem("ws"), h * 8 + (c + 1))
                        done(V.tensor_tensor(vnew[r, :], us[r, t, :], bank[5][r, 0:P], ALU.subtract), "vnew", h * 8 + (c + 1))
                    if side:
                        side.pop(0)()
                    if delta:
                        dve.wait_ge(sem("kv"), h * 8 + (c + 1))
                        last = 64 * (c % 2) + 63
                        done(V.scalar_tensor_tensor(out=state[:, :], in0=state[:, :], scalar=eg[:, t, last:last + 1],
                                                    in1=bank[7][:, 0:P], op0=ALU.mult, op1=ALU.add),
                             "state", h * 9 + (c + 2))
                    if c == 1 and more_a:
                        prep(h + 2, 1)
                    if c == 4 and attention:
                        dve.wait_ge(sem("oa_r"), a + 1)
                        done(V.scalar_tensor_tensor(out=dyn(o_a, a),
                                                    in0=bank[3][:, :], scalar=gsub, in1=pr[1][:, :],
                                                    op0=ALU.mult, op1=ALU.mult), "oa_done", a + 2)
                    if c in (1, 2, 3, 5, 6) and side:
                        side.pop(0)()
                steps(side)
                if delta:
                    dve.wait_ge(sem("ob_sq"), h + 1)
                    link(V.scalar_tensor_tensor(out=dyn(o_b, h), in0=bank[6][:, :], scalar=col(PA_ON), in1=zb[:, :],
                                                op0=ALU.mult, op1=ALU.mult))
                if attention:
                    head_start(a)
                if delta:
                    dve.wait_ge(sem("ob_r"), h + 1)
                    done(V.tensor_tensor(dyn(o_b, h), dyn(o_b, h), sqo[:, :], ALU.mult), "ob_done", h + 2)

            def low_a(chunks):
                for k in chunks:
                    dve.wait_ge(sem("o_high"), k + 1)
                    done(V.tensor_tensor(oa_lo[:, k, :], o_a[:, k, :], oa_hi[:, k, :].bitcast(F32), ALU.subtract),
                         "o_split", k + 1)

            def mix_a(n, c, gate):
                dve.wait_ge(sem("ga_made"), n + 1)
                dve.wait_ge(product_ready, c.number + 1)
                done(V.tensor_tensor(dyn(o_a, n), gate[:, :], bank[c.bank][:, :], ALU.mult), bank_free[c.bank], c.uses + 1)
                dve.sem_inc(sem("ga_used"), 1)

            def g_steps(h):
                def one(n, dst, g):
                    done(V.tensor_scalar(dst[:, :, :], gcols(g, h).to_broadcast([P, NT, P]), 1.0, None, ALU.mult),
                         "g_cols", h * 2 + (n + 1))
                return [lambda: one(0, gcol, G_CUM), lambda: one(1, bcol, G_BETA)]

            def place(seg, names, h=0):
                return lambda name: seg.at(names.index(name), h)

            def head_turn(h):
                turn(h, place(stream.heads, TURN, h), stream.heads.at(TURN.index("vb"), h - 1))

            prep(0, 0)
            prep(0, 1)
            turn(-1, place(stream.lead, LEAD), None, delta=False)
            LINKS = {head_turn: 48}
            loop(H - 2, head_turn)
            turn(H - 2, place(stream.late, LATE), stream.heads.at(TURN.index("vb"), H - 3), more_a=False)
            turn(H - 1, None, stream.late.at(3), attention=False, more_a=False)

            mix_a(2, stream.mix_a.at(2, 1), sqr[0])
            mix_a(3, stream.mix_a.at(3, 1), sqr[1])
            for k in range(H):
                dve.wait_ge(sem("o_high"), H + k + 1)
                done(V.tensor_tensor(ob_lo[:, k, :], o_b[:, k, :], ob_hi[:, k, :].bitcast(F32), ALU.subtract),
                     "o_split", H + k + 1)

            def mix_a_turn(n):
                for q in range(2):
                    mix_a(n * 2 + (4 + q), stream.mix_a.at(2 + q, n + 2), sg[q])

            LINKS[mix_a_turn] = 0
            loop(KD // 2 - 2, mix_a_turn)

            def mix_b_turn(n):
                for q in range(2):
                    c, k = stream.mix_b.at(2 + q, n), n * 2 + q
                    dve.wait_ge(sem("gb_made"), n * 2 + (q + 1))
                    dve.wait_ge(product_ready, c.number + 1)
                    done(V.tensor_tensor(sg[q][:, :], sg[q][:, :], bank[c.bank][:, :], ALU.mult), bank_free[c.bank], c.uses + 1)
                    link(V.tensor_tensor(sg[q][:, :], sg[q][:, :], dyn(o_a, k), ALU.add))
                    link(V.tensor_scalar(dyn(mx_hi, k), sg[q][:, :], 1.0, None, ALU.mult))
                    link(V.tensor_tensor(dyn(mx_lo, k), sg[q][:, :], dyn(mx_hi, k).bitcast(F32), ALU.subtract))
                    dve.sem_inc(sem("gb_used"), 1)

            LINKS[mix_b_turn] = 6
            loop(KD // 2, mix_b_turn)

            def low(stage, c, gain):
                dve.wait_ge(sem("n_high"), stage * KD + c + 1)
                done(V.scalar_tensor_tensor(out=hn_lo[:, c, :], in0=x1[:, c, :], scalar=pt[:, gain + c:gain + c + 1],
                                            in1=hn_hi[:, c, :].bitcast(F32), op0=ALU.mult, op1=ALU.subtract),
                     "n_split", stage * KD + c + 1)

            for c in range(KD):
                low(0, c, PA_FFN)
            dve.wait_ge(sem("n_r"), 1)

            def up_turn(part):
                def body(n):
                    for pair in range(2):
                        f = n * 2 + (FFN_FIRST[part] + pair)
                        for q, u in ((0, u0), (1, u1)):
                            c = stream.up[part].at(2 * pair + q, n)
                            src = bank[c.bank]

                            def tap(j):
                                return col(PA_TAP[j] + q * KF, f)
                            dve.wait_ge(product_ready, c.number + 1)
                            done(V.tensor_tensor(vr[:, :], src[:, :], rs[:, :], ALU.mult), bank_free[c.bank], c.uses + 1)
                            link(V.tensor_scalar(u[:, :], vr[:, :], tap(2), col(PA_FBIAS + q * KF, f), ALU.mult, ALU.add))
                            for j, back in ((1, 1), (0, 2)):
                                link(V.scalar_tensor_tensor(out=u[:, back:], in0=vr[:, 0:T - back], scalar=tap(j),
                                                            in1=u[:, back:], op0=ALU.mult, op1=ALU.add))
                            if q == 0:
                                dve.sem_inc(sem("u_conv"), 1)
                        dve.wait_ge(sem("u_sig"), f + 1)
                        link(V.tensor_tensor(tn[:, :], u0[:, :], s0[:, :], ALU.mult))
                        link(V.tensor_tensor(tn[:, :], tn[:, :], u1[:, :], ALU.mult))
                        k = n * 2 + (8 * FFN_HALF[part] + pair)
                        link(V.tensor_scalar(dyn(fa_hi, k), tn[:, :], 1.0, None, ALU.mult))
                        done(V.tensor_tensor(dyn(fa_lo, k), tn[:, :], dyn(fa_hi, k).bitcast(F32), ALU.subtract),
                             "fa_lo", f + 1)
                LINKS[body] = 18
                return body

            for name, part in FFN_ORDER:
                if name == "up":
                    if part == 2:
                        dve.wait_ge(product_ready, stream.up[2].first)
                    loop(FFN_PARTS[part] // 2, up_turn(part))
                    if part == 0:
                        for c in range(KP):
                            dve.wait_ge(sem("p_high"), c + 1)
                            done(V.tensor_tensor(p_lo[:, c, :], bank[5 + c][:, :], p_hi[:, c, :].bitcast(F32), ALU.subtract),
                                 "p_split", c + 1)
                else:
                    def down_turn(n, part=part):
                        for q in range(4):
                            c = stream.down[part].at(q, n)
                            dve.wait_ge(product_ready, c.number + 1)
                            k = n * 4 + q
                            link(V.tensor_tensor(dyn(x1, k), dyn(x1, k), bank[c.bank][:, :], ALU.add))
                            dve.sem_inc(bank_free[c.bank], 1)
                    if part < 2:
                        LINKS[down_turn] = 4
                        loop(KD // 4, down_turn)
                    else:
                        for k in range(KD):
                            c = stream.down[part].at(k)
                            dve.wait_ge(product_ready, c.number + 1)
                            done(V.tensor_tensor(x1[:, k, :], x1[:, k, :], bank[c.bank][:, :], ALU.add),
                                 bank_free[c.bank], c.uses + 1)
                            gain = pt[:, PA_PLE + k:PA_PLE + k + 1]
                            link(V.tensor_scalar(hn_hi[:, k, :], x1[:, k, :], gain, None, ALU.mult))
                            done(V.scalar_tensor_tensor(out=hn_lo[:, k, :], in0=x1[:, k, :], scalar=gain,
                                                        in1=hn_hi[:, k, :].bitcast(F32), op0=ALU.mult,
                                                        op1=ALU.subtract), "n_split", KD + k + 1)
                            if k >= 2:
                                dve.wait_ge(sem("n_sum"), KD + k - 1)
                            done(V.tensor_tensor((s0, tn)[k % 2][:, :], x1[:, k, :], x1[:, k, :], ALU.mult),
                                 "n_sq", KD + k + 1)

            def gated(n, q):
                k = n * 2 + q
                g, c = stream.ple.at(2 * q, n), stream.ple.at(2 * q + 1, n)
                dve.wait_ge(product_ready, g.number + 1)
                done(V.tensor_tensor(yg[:, :], bank[g.bank][:, :], rs[:, :], ALU.mult), bank_free[g.bank], g.uses + 1)
                dve.sem_inc(sem("gate_scaled"), 1)
                if not isinstance(k, int) or k > 0:
                    turned_y(k - 1)
                y = yT[q % 2]
                dve.wait_ge(sem("gate"), k + 1)
                dve.wait_ge(product_ready, c.number + 1)
                done(V.tensor_tensor(y[:, :], yg[:, :], bank[c.bank][:, :], ALU.mult), bank_free[c.bank], c.uses + 1)
                done(V.tensor_tensor(y[:, :], y[:, :], dyn(x1, k), ALU.add), "yT", k + 2)

            def turned_y(k):
                dve.wait_ge(sem("y_T"), k + 1)
                done(V.tensor_scalar(y_tok[:, :, bass.ds(k * P, P)], tiles(5), 1.0, None, ALU.mult), "y_ready", k + 1)

            def ple_turn(n):
                gated(n, 1)
                gated(n, 2)

            dve.wait_ge(sem("n_r"), 2)
            gated(0, 0)
            LINKS[ple_turn] = 0
            loop(KD // 2 - 1, ple_turn)
            gated(KD // 2 - 1, 1)
            turned_y(KD - 1)


_INS = ["x", "p", "w_in", "attn_norm", "qnorm_a", "knorm_a", "lam_a", "subln_a", "rel_bias", "conv_b",
        "a_log_b", "dt_bias_b", "onorm_b", "w_br_a", "w_br_b", "w_out", "ffn_norm", "w_up", "conv_ff",
        "conv_ff_bias", "w_down", "ple_norm", "w_ple_gate", "w_ple_proj"]


def kernel(**inputs):
    import concourse.bacc as bacc
    from concourse.bass_utils import run_bass_kernel_spmd

    nc = bacc.Bacc("TRN2", target_bir_lowering=False, num_devices=1)
    arrays = {f"in_{name}": np.ascontiguousarray(inputs[name]) for name in _INS}
    arrays["in_consts"] = constants()
    args = [nc.dram_tensor(n, a.shape, mybir.dt.from_np(a.dtype), kind="ExternalInput").ap()
            for n, a in arrays.items()]
    args.append(nc.dram_tensor("out_0", (1, T, D), F32, kind="ExternalOutput").ap())
    build(nc, *args)
    r = run_bass_kernel_spmd(nc, [arrays], core_ids=[0])
    return r.results[0]["out_0"]
```
